# Optimizing a Trainium2 kernel written in Bass

```python
import jax, jax.numpy as jnp
from jax import lax
import numpy as np

D_MODEL = 1024
BATCH = 1
SEQ = 512
DEPTH = 1

CHUNK = 64
EPS = 1e-6
GMLP_BLOCK = 128
GMLP_GROUPS = 4
GMLP_GROUP_DIM = 128
GMLP_WIDTH = GMLP_GROUPS * GMLP_GROUP_DIM
HG_HEADS = 8
HG_DK = 128
HG_DV = D_MODEL // HG_HEADS
HG_WIDTH = HG_HEADS * HG_DK
HG_VWIDTH = HG_HEADS * HG_DV
N_BRANCH = 2
D_FF = 4 * D_MODEL
IN_SPLITS = (GMLP_WIDTH, GMLP_WIDTH, HG_WIDTH, HG_WIDTH, HG_VWIDTH, HG_VWIDTH, D_MODEL, D_MODEL)
IN_COLS = sum(IN_SPLITS)


def rmsnorm(x, g):
    xf = x.astype(jnp.float32)
    y = xf * lax.rsqrt(jnp.mean(xf * xf, axis=-1, keepdims=True) + EPS)
    return (y * g.astype(jnp.float32)).astype(x.dtype)

def layernorm(x, g, b):
    xf = x.astype(jnp.float32)
    mu = jnp.mean(xf, axis=-1, keepdims=True)
    xc = xf - mu
    y = xc * lax.rsqrt(jnp.mean(xc * xc, axis=-1, keepdims=True) + EPS)
    return (y * g.astype(jnp.float32) + b.astype(jnp.float32)).astype(x.dtype)

def chunk_causal_mask(n):
    c = jnp.arange(n) // CHUNK
    return c[None, :] <= c[:, None]

def gmlp_branch(zu, zv, ln_g, ln_b, w_s, b_s):
    B, S, _ = zu.shape
    nb = S // GMLP_BLOCK
    u = jax.nn.gelu(zu, approximate=False)
    v = layernorm(jax.nn.gelu(zv, approximate=False), ln_g, ln_b)
    v = v.reshape(B, nb, GMLP_BLOCK, GMLP_GROUPS, GMLP_GROUP_DIM)
    w = jnp.where(chunk_causal_mask(GMLP_BLOCK)[None], w_s, 0).astype(v.dtype)
    mixed = jnp.einsum('gqp,bnpgc->bnqgc', w, v) + b_s.T.astype(v.dtype)[None, None, :, :, None]
    return u * mixed.reshape(B, S, GMLP_WIDTH)

def hgrn2_lower_bounds(lb_param):
    p = jax.nn.softmax(lb_param.astype(jnp.float32), axis=0)
    return jnp.cumsum(p, axis=0) - p[0]

def hgrn2_chunkwise(q, k, v, log_f):
    B, S, H, DK = q.shape
    DV = v.shape[-1]
    nc = S // CHUNK

    def to_chunks(t):
        return t.reshape(B, nc, CHUNK, H, t.shape[-1]).transpose(1, 0, 3, 2, 4)

    tri = jnp.tril(jnp.ones((CHUNK, CHUNK), dtype=bool))[:, :, None]

    def step(state, inp):
        qb, kb, vb, gb = inp
        cum = jnp.cumsum(gb, axis=2)
        o_inter = jnp.einsum('bhtk,bhkv->bhtv', qb * jnp.exp(cum), state)
        rel = cum[:, :, :, None, :] - cum[:, :, None, :, :]
        decay = jnp.exp(jnp.where(tri, rel, -jnp.inf))
        scores = jnp.einsum('bhtk,bhsk,bhtsk->bhts', qb, kb, decay)
        o_intra = jnp.einsum('bhts,bhsv->bhtv', scores, vb)
        last = cum[:, :, -1:, :]
        k_dec = kb * jnp.exp(last - cum)
        state = state * jnp.exp(last[:, :, 0, :])[..., None] + jnp.einsum('bhsk,bhsv->bhkv', k_dec, vb)
        return state, o_inter + o_intra

    state0 = jnp.zeros((B, H, DK, DV), jnp.float32)
    _, out = lax.scan(step, state0, (to_chunks(q), to_chunks(k), to_chunks(v), to_chunks(log_f)))
    return out.transpose(1, 0, 3, 2, 4).reshape(B, S, H, DV)

def hgrn2_branch(zq, zf, zi, zo, lb, layer_idx, norm_g):
    B, S, _ = zq.shape
    dt = zq.dtype
    zf32 = zf.astype(jnp.float32)
    if layer_idx == 0:
        log_f = jax.nn.log_sigmoid(zf32)
        k = jax.nn.sigmoid(-zf32)
    else:
        f = lb[None, None, :] + (1.0 - lb[None, None, :]) * jax.nn.sigmoid(zf32)
        log_f = jnp.log(f)
        k = 1.0 - f
    q = jax.nn.silu(zq.astype(jnp.float32))
    heads = lambda t, d: t.reshape(B, S, HG_HEADS, d)
    o = hgrn2_chunkwise(heads(q, HG_DK), heads(k, HG_DK),
                        heads(zi.astype(jnp.float32), HG_DV), heads(log_f, HG_DK))
    o = rmsnorm(o, norm_g) * jax.nn.silu(heads(zo.astype(jnp.float32), HG_DV))
    return o.reshape(B, S, HG_VWIDTH).astype(dt)

def first_inputs(seed: int = 0) -> dict:
    key = jax.random.key(seed)
    ks = jax.random.split(key, 16)
    n = jax.random.normal
    f32 = jnp.float32
    return {
        "x": n(ks[0], (BATCH, SEQ, D_MODEL), f32),
        "w_in": n(ks[1], (DEPTH, D_MODEL, IN_COLS), f32) * D_MODEL ** -0.5,
        "gmlp_ln_g": 1.0 + 0.05 * n(ks[2], (DEPTH, GMLP_WIDTH), f32),
        "gmlp_ln_b": 0.02 * n(ks[3], (DEPTH, GMLP_WIDTH), f32),
        "gmlp_ws": n(ks[4], (DEPTH, GMLP_GROUPS, GMLP_BLOCK, GMLP_BLOCK), f32) * GMLP_BLOCK ** -0.5,
        "gmlp_bs": 1.0 + 0.05 * n(ks[5], (DEPTH, GMLP_GROUPS, GMLP_BLOCK), f32),
        "w_up_a": n(ks[6], (DEPTH, GMLP_WIDTH, D_MODEL), f32) * GMLP_WIDTH ** -0.5,
        "hg_lb": 0.5 * n(ks[7], (DEPTH, HG_WIDTH), f32),
        "hg_norm_g": 1.0 + 0.05 * n(ks[8], (DEPTH, HG_DV), f32),
        "w_up_b": n(ks[9], (DEPTH, HG_VWIDTH, D_MODEL), f32) * HG_VWIDTH ** -0.5,
        "w_out": n(ks[10], (DEPTH, D_MODEL, D_MODEL), f32) * D_MODEL ** -0.5,
        "norm_mix": 1.0 + 0.05 * n(ks[11], (DEPTH, D_MODEL), f32),
        "norm_ffn": 1.0 + 0.05 * n(ks[12], (DEPTH, D_MODEL), f32),
        "w_ff1": n(ks[13], (DEPTH, D_MODEL, D_FF), f32) * D_MODEL ** -0.5,
        "w_ff2": n(ks[14], (DEPTH, D_FF, D_MODEL), f32) * (0.5 * D_FF ** -0.5),
        "final_norm": 1.0 + 0.05 * n(ks[15], (D_MODEL,), f32),
    }

def first_block(x, w_in, gmlp_ln_g, gmlp_ln_b, gmlp_ws, gmlp_bs, w_up_a, hg_lb, hg_norm_g,
              w_up_b, w_out, norm_mix, norm_ffn, w_ff1, w_ff2, final_norm):
    split_points = [int(s) for s in np.cumsum(IN_SPLITS)[:-1]]
    lower_bounds = hgrn2_lower_bounds(hg_lb)
    for l in range(DEPTH):
        h = rmsnorm(x, norm_mix[l])
        proj = h @ w_in[l]
        zu, zv, zq, zf, zi, zo, g_a, g_b = jnp.split(proj, split_points, axis=-1)
        y_a = gmlp_branch(zu, zv, gmlp_ln_g[l], gmlp_ln_b[l], gmlp_ws[l], gmlp_bs[l]) @ w_up_a[l]
        y_b = hgrn2_branch(zq, zf, zi, zo, lower_bounds[l], l, hg_norm_g[l]) @ w_up_b[l]
        mix = jax.nn.sigmoid(g_a) * y_a + jax.nn.sigmoid(g_b) * y_b
        x = x + mix @ w_out[l]
        h = rmsnorm(x, norm_ffn[l])
        x = x + jnp.square(jax.nn.relu(h @ w_ff1[l])) @ w_ff2[l]
    return rmsnorm(x, final_norm)


DEPTH_2 = 2

N_MIXERS = 2
CONV_K = 4
M_INNER = 2 * D_MODEL
M_HEADS = 4
M_DV = M_INNER // M_HEADS
M_DK = M_DV // 2
M_CHUNK = 64
R_WIDTH = 3 * D_MODEL // 2
R_BLOCKS = 8
R_BS = R_WIDTH // R_BLOCKS
LRU_C = 8.0

N_A = (DEPTH_2 + 1) // 2
N_B = DEPTH_2 // 2


def rmsnorm_2(x, g):
    xf = x.astype(jnp.float32)
    y = xf * lax.rsqrt(jnp.mean(xf * xf, axis=-1, keepdims=True) + EPS)
    return (y * g.astype(jnp.float32)).astype(x.dtype)

def causal_dwconv(x, w, b):
    s = x.shape[1]
    xp = jnp.pad(x, ((0, 0), (CONV_K - 1, 0), (0, 0)))
    y = b + xp[:, 0:s] * w[0]
    for j in range(1, CONV_K):
        y = y + xp[:, j:j + s] * w[j]
    return y

def mlstm_chunkwise(q, k, v, log_i, log_f):
    b, h, s, dk = q.shape
    dv = v.shape[-1]
    L = M_CHUNK
    nc = s // L

    def to_chunks(t):
        t = t.reshape((b, h, nc, L) + t.shape[3:])
        return jnp.moveaxis(t, 2, 0)

    qc, kc, vc, ic, fc = (to_chunks(t) for t in (q, k, v, log_i, log_f))
    causal = jnp.tril(jnp.ones((L, L), dtype=bool))

    def step(carry, inp):
        C, n, m = carry
        qb, kb, vb, ib, fb = inp
        F = jnp.cumsum(fb, axis=-1)
        D = F[..., :, None] - F[..., None, :] + ib[..., None, :]
        D = jnp.where(causal, D, -jnp.inf)
        m_t = jnp.maximum(F + m[..., None], jnp.max(D, axis=-1))
        decay = jnp.exp(F + m[..., None] - m_t)
        W = jnp.exp(D - m_t[..., None])
        Sm = jnp.einsum('bhtk,bhsk->bhts', qb, kb) * W
        num = (decay[..., None] * jnp.einsum('bhtk,bhkv->bhtv', qb, C)
               + jnp.einsum('bhts,bhsv->bhtv', Sm, vb))
        den = decay * jnp.einsum('bhtk,bhk->bht', qb, n) + jnp.sum(Sm, axis=-1)
        hb = num / jnp.maximum(jnp.abs(den), jnp.exp(-m_t))[..., None]
        w_last = W[..., -1, :]
        d_last = decay[..., -1]
        C_new = d_last[..., None, None] * C + jnp.einsum('bhs,bhsk,bhsv->bhkv', w_last, kb, vb)
        n_new = d_last[..., None] * n + jnp.einsum('bhs,bhsk->bhk', w_last, kb)
        return (C_new, n_new, m_t[..., -1]), hb

    init = (jnp.zeros((b, h, dk, dv), jnp.float32),
            jnp.zeros((b, h, dk), jnp.float32),
            jnp.zeros((b, h), jnp.float32))
    _, hs = lax.scan(step, init, (qc, kc, vc, ic, fc))
    return jnp.moveaxis(hs, 0, 2).reshape(b, h, s, dv)

def mlstm_mixer(u, w_in, conv_w, conv_b, w_q, w_k, w_v, b_i, b_f, norm_w, skip, w_out):
    bsz, s, _ = u.shape
    proj = u @ w_in
    xm, z, o_pre, i_pre, f_pre = jnp.split(
        proj, [M_INNER, 2 * M_INNER, 3 * M_INNER, 3 * M_INNER + M_HEADS], axis=-1)
    xc = jax.nn.silu(causal_dwconv(xm, conv_w, conv_b))
    xch = xc.reshape(bsz, s, M_HEADS, M_DV)
    xmh = xm.reshape(bsz, s, M_HEADS, M_DV)
    q = jnp.einsum('bshd,hde->bhse', xch, w_q).astype(jnp.float32) * (M_DK ** -0.5)
    k = jnp.einsum('bshd,hde->bhse', xch, w_k).astype(jnp.float32)
    v = jnp.einsum('bshd,hde->bhse', xmh, w_v).astype(jnp.float32)
    log_i = jnp.transpose((i_pre + b_i).astype(jnp.float32), (0, 2, 1))
    log_f = jnp.transpose(jax.nn.log_sigmoid((f_pre + b_f).astype(jnp.float32)), (0, 2, 1))
    h_tilde = jnp.transpose(mlstm_chunkwise(q, k, v, log_i, log_f), (0, 2, 1, 3))
    o = jax.nn.sigmoid(o_pre.astype(jnp.float32)).reshape(bsz, s, M_HEADS, M_DV)
    hh = o * h_tilde
    mu = jnp.mean(hh, axis=-1, keepdims=True)
    var = jnp.mean(jnp.square(hh - mu), axis=-1, keepdims=True)
    hn = ((hh - mu) * lax.rsqrt(var + EPS)).reshape(bsz, s, M_INNER)
    hn = (hn * norm_w.astype(jnp.float32)).astype(u.dtype)
    y = (hn + skip * xc) * jax.nn.silu(z)
    return y @ w_out

def linear_scan(a, bt):
    def step(hc, ab):
        a_t, b_t = ab
        hc = a_t * hc + b_t
        return hc, hc
    h0 = jnp.zeros((a.shape[0], a.shape[2]), jnp.float32)
    _, hs = lax.scan(step, h0, (jnp.moveaxis(a, 1, 0), jnp.moveaxis(bt, 1, 0)))
    return jnp.moveaxis(hs, 0, 1)

def rglru_mixer(u, w_in, conv_w, conv_b, w_a, b_a, w_x, b_x, lam, w_out):
    bsz, s, _ = u.shape
    proj = u @ w_in
    xr, g = jnp.split(proj, [R_WIDTH], axis=-1)
    xc = causal_dwconv(xr, conv_w, conv_b)
    xb = xc.reshape(bsz, s, R_BLOCKS, R_BS)
    r = jax.nn.sigmoid(jnp.einsum('bsnc,ncd->bsnd', xb, w_a).reshape(bsz, s, R_WIDTH) + b_a)
    ig = jax.nn.sigmoid(jnp.einsum('bsnc,ncd->bsnd', xb, w_x).reshape(bsz, s, R_WIDTH) + b_x)
    log_a = -LRU_C * r.astype(jnp.float32) * jax.nn.softplus(-lam.astype(jnp.float32))
    a = jnp.exp(log_a)
    bt = jnp.sqrt(-jnp.expm1(2.0 * log_a)) * (ig * xc).astype(jnp.float32)
    hs = linear_scan(a, bt).astype(u.dtype)
    y = hs * jax.nn.silu(g)
    return y @ w_out

def second_inputs(seed: int = 0) -> dict:
    key = jax.random.key(seed)
    ks = iter(jax.random.split(key, 32))
    nrm = lambda shape, scale: jax.random.normal(next(ks), shape, jnp.float32) * scale
    i_w = 3 * M_INNER + 2 * M_HEADS
    lam_u = jax.random.uniform(next(ks), (N_B, R_WIDTH), jnp.float32, 0.9, 0.999)
    sig = lam_u ** (1.0 / LRU_C)
    b_f = jnp.broadcast_to(jnp.linspace(3.0, 6.0, M_HEADS, dtype=jnp.float32), (N_A, M_HEADS))
    return {
        "x": nrm((BATCH, SEQ, D_MODEL), 1.0),
        "ln_g": 1.0 + nrm((DEPTH_2, D_MODEL), 0.05),
        "final_g": 1.0 + nrm((D_MODEL,), 0.05),
        "m_w_in": nrm((N_A, D_MODEL, i_w), D_MODEL ** -0.5),
        "m_conv_w": nrm((N_A, CONV_K, M_INNER), CONV_K ** -0.5),
        "m_conv_b": nrm((N_A, M_INNER), 0.02),
        "m_w_q": nrm((N_A, M_HEADS, M_DV, M_DK), M_DV ** -0.5),
        "m_w_k": nrm((N_A, M_HEADS, M_DV, M_DK), M_DV ** -0.5),
        "m_w_v": nrm((N_A, M_HEADS, M_DV, M_DV), M_DV ** -0.5),
        "m_b_i": nrm((N_A, M_HEADS), 0.1),
        "m_b_f": b_f + nrm((N_A, M_HEADS), 0.1),
        "m_norm_w": 1.0 + nrm((N_A, M_INNER), 0.05),
        "m_skip": 1.0 + nrm((N_A, M_INNER), 0.05),
        "m_w_out": nrm((N_A, M_INNER, D_MODEL), M_INNER ** -0.5),
        "r_w_in": nrm((N_B, D_MODEL, 2 * R_WIDTH), D_MODEL ** -0.5),
        "r_conv_w": nrm((N_B, CONV_K, R_WIDTH), CONV_K ** -0.5),
        "r_conv_b": nrm((N_B, R_WIDTH), 0.02),
        "r_w_a": nrm((N_B, R_BLOCKS, R_BS, R_BS), R_BS ** -0.5),
        "r_b_a": nrm((N_B, R_WIDTH), 0.02),
        "r_w_x": nrm((N_B, R_BLOCKS, R_BS, R_BS), R_BS ** -0.5),
        "r_b_x": nrm((N_B, R_WIDTH), 0.02),
        "r_lam": jnp.log(sig / (1.0 - sig)),
        "r_w_out": nrm((N_B, R_WIDTH, D_MODEL), R_WIDTH ** -0.5),
    }

def second_block(x, ln_g, final_g, m_w_in, m_conv_w, m_conv_b, m_w_q, m_w_k, m_w_v, m_b_i, m_b_f,
              m_norm_w, m_skip, m_w_out, r_w_in, r_conv_w, r_conv_b, r_w_a, r_b_a, r_w_x, r_b_x,
              r_lam, r_w_out):
    for layer in range(DEPTH_2):
        u = rmsnorm_2(x, ln_g[layer])
        j = layer // N_MIXERS
        if layer % N_MIXERS == 0:
            y = mlstm_mixer(u, m_w_in[j], m_conv_w[j], m_conv_b[j], m_w_q[j], m_w_k[j], m_w_v[j],
                            m_b_i[j], m_b_f[j], m_norm_w[j], m_skip[j], m_w_out[j])
        else:
            y = rglru_mixer(u, r_w_in[j], r_conv_w[j], r_conv_b[j], r_w_a[j], r_b_a[j],
                            r_w_x[j], r_b_x[j], r_lam[j], r_w_out[j])
        x = x + y
    return rmsnorm_2(x, final_g)


def setup_inputs(seed=0):
    out = dict(first_inputs(seed))
    for name, value in second_inputs(seed + 1).items():
        if name != "x":
            out[name + "_2"] = value
    return out


def reference(
    x, w_in, gmlp_ln_g, gmlp_ln_b, gmlp_ws, gmlp_bs, w_up_a, hg_lb, hg_norm_g, w_up_b, w_out,
    norm_mix, norm_ffn, w_ff1, w_ff2, final_norm, ln_g_2, final_g_2, m_w_in_2, m_conv_w_2,
    m_conv_b_2, m_w_q_2, m_w_k_2, m_w_v_2, m_b_i_2, m_b_f_2, m_norm_w_2, m_skip_2, m_w_out_2,
    r_w_in_2, r_conv_w_2, r_conv_b_2, r_w_a_2, r_b_a_2, r_w_x_2, r_b_x_2, r_lam_2, r_w_out_2,
):
    x = first_block(
        x, w_in, gmlp_ln_g, gmlp_ln_b, gmlp_ws, gmlp_bs, w_up_a, hg_lb, hg_norm_g, w_up_b,
        w_out, norm_mix, norm_ffn, w_ff1, w_ff2, final_norm,
    )
    return second_block(
        x, ln_g_2, final_g_2, m_w_in_2, m_conv_w_2, m_conv_b_2, m_w_q_2, m_w_k_2, m_w_v_2,
        m_b_i_2, m_b_f_2, m_norm_w_2, m_skip_2, m_w_out_2, r_w_in_2, r_conv_w_2, r_conv_b_2,
        r_w_a_2, r_b_a_2, r_w_x_2, r_b_x_2, r_lam_2, r_w_out_2,
    )


_drawn_inputs = setup_inputs


def setup_inputs(seed=0):
    import zlib

    import numpy as np

    out = dict(_drawn_inputs(seed))
    spreads = {}
    factors = {'gmlp_ln_g': 2.756,
     'gmlp_ln_b': 7.13,
     'm_b_i_2': 64.0,
     'm_skip_2': 3.602,
     'r_b_a_2': 49.057,
     'r_b_x_2': 24.757,
     'gmlp_bs': 2.86,
     'hg_norm_g': 3.04,
     'm_norm_w_2': 3.03}
    for name, (base, spread) in spreads.items():
        noise = np.random.default_rng([zlib.crc32(name.encode()), seed]).standard_normal(out[name].shape)
        drawn = base * np.exp(spread * noise) if base else spread * noise
        out[name] = __import__('jax').numpy.asarray(drawn.astype(out[name].dtype))
    for name, factor in factors.items():
        out[name] = (out[name] * factor).astype(out[name].dtype)
    return out
```

```python
from contextlib import ExitStack

import concourse.bass as bass
from concourse import mybir

F32 = mybir.dt.float32
F32R = mybir.dt.float32r
U8 = mybir.dt.uint8
ALU = mybir.AluOpType
ACT = mybir.ActivationFunctionType

P = 128
S = 512
NT = S // P
D = 1024
DT = D // P
EPS = 1e-6
RING = 4
PANEL = 8 * P
CHUNK = 64
NCH = S // CHUNK

GG = 4
HH = 8
LEVELS = [1, 2, 4, 8, 16, 32, 64, 128, 256]
NMASK = 8
M_BANK = [4, 5, 5, 6, 6, 7, 7, 4]
M_AT = [0, 0, 256, 0, 256, 0, 256, 0]
M_FREED = {0: 1, 2: 1, 4: 1, 6: 2, 7: 2}
M_TURNS = NMASK + NMASK - len(M_FREED)
MH = 4
MT = 4
MQ = 2
RG = 4
RT = 3
RW = 1536

G_P, G_T = 0, 0
H_P, H_T, H_N = 8, 8, 4
U_P, U_T, U_N = 40, 40, 8
O_P, O_T = 72, 72
F_P, F_T, F_N = 80, 80, 16
M_P, M_NP, M_T, M_NT = 144, 20, 144, 32
R_P, R_NP, R_T, R_NT = 224, 10, 272, 20
N_PANELS = 264

AUX_G = {4: 4, 5: 3, 6: 3, 7: 3}
AUX_H = {4: 6, 5: 5, 6: 5, 7: 5}
H_AUX = {4: 3, 5: 2, 6: 2, 7: 3}
AUX_N1 = {b: AUX_H[b] + HH * H_AUX[b] for b in H_AUX}
AUX_N2 = {**AUX_N1, 4: AUX_N1[4] + 1}
AUX_MP = {**AUX_N2, 4: AUX_N2[4] + 2}
AUX_M = {4: AUX_MP[4], 5: AUX_MP[5] + 1, 6: AUX_MP[6] + 1, 7: AUX_MP[7] + 1}
AUX_N3 = {b: AUX_M[b] + MH * 2 for b in AUX_M}
AUX_N4 = {**AUX_N3, 4: AUX_N3[4] + 1}
AUX_E = {**AUX_N4, 4: AUX_N4[4] + 1}
NORM_AUX = [3, AUX_N1[4], AUX_N2[4], AUX_N2[4] + 1, AUX_N3[4], AUX_N4[4]]

ROWS = {}


def plan_rows():
    for sheet, names in enumerate([
        [("norm_mix", 8), ("norm_ffn", 8), ("final_norm", 8), ("ln_g_2", 16), ("final_g_2", 8), ("hg_norm_g", 1),
         ("r_lam_2", 12), ("r_b_a_2", 12), ("r_b_x_2", 12), ("r_conv_b_2", 12)],
        [("m_conv_w_2", 64), ("m_conv_b_2", 16), ("m_norm_w_2", 16), ("m_skip_2", 16)],
        [("r_conv_w_2", 48)],
    ]):
        at = 0
        for name, n in names:
            ROWS[name] = (sheet, at, n)
            at += n
        assert at <= P


plan_rows()
SHEET_ROWS = [max(at + n for s, at, n in ROWS.values() if s == sheet) for sheet in range(3)]


class Steps:

    def __init__(self, eng, sem):
        self.eng, self.sem, self.n = eng, sem, 0

    def link(self, ins):
        self.n = self.n + 1
        ins.then_inc(self.sem, 1)
        self.eng.wait_ge(self.sem, self.n)

    def loop(self, turns, per, body, first=0):
        start = self.n
        with self.eng.Fori(0, turns) as i:
            self.n = start + i * per
            before = [0]
            count = Counted(self)
            body(i + first if first else i)
            assert count.taken() == per, (count.taken(), per)
        self.n = start + turns * per


class Counted:
    def __init__(self, steps):
        self.steps, self.made, self.real = steps, 0, steps.link

        def link(ins):
            self.made += 1
            self.real(ins)
        steps.link = link

    def taken(self):
        self.steps.link = self.real
        return self.made


def two_blocks(nc, A, out, stop=None):
    ctx = ExitStack()
    with ctx:
        def sem(name):
            return ctx.enter_context(nc.semaphore(name))

        place = [(nc.sbuf_base + 63) // 64 * 64]

        def sb(name, shape, dt, at=None):
            size = 1
            for n in shape[1:]:
                size *= n
            size = (size * (1 if dt == U8 else 4) + 31) // 32 * 32
            if at is None:
                at = place[0]
                place[0] += size
            else:
                at, place_end = at[0], at
                place_end[0] += size
            return nc.alloc_sbuf_tensor_at(name, shape, dt, offset=at)

        raw = sb("raw", [P, RING, PANEL], F32)
        w_hi = sb("w_hi", [P, RING, PANEL], F32R)
        w_lo = sb("w_lo", [P, RING, PANEL], F32R)
        xT = sb("xT", [P, DT, S], F32)
        h_hi = sb("h_hi", [P, DT, S], F32R)
        h_lo = sb("h_lo", [P, DT, S], F32R)
        ident = sb("ident", [P, P], F32)
        ones = sb("ones", [P, P], F32)
        ones_m = sb("ones_m", [P, P], F32)
        cols = sb("cols", [P, 3, P], F32)
        mask4_at = place[0]
        mask4 = sb("mask4", [P, NMASK, 2 * P], U8)
        mask_d = sb("mask_d", [P, 1, P], U8)
        keep = sb("keep", [P, S], F32)
        cap = sb("cap", [P, P], F32)
        sq = sb("sq", [P, 2, S], F32)
        rstd = sb("rstd", [P, S], F32)
        hf = sb("hf", [P, 2, S], F32)
        small = sb("small", [P, 16], F32)
        sel = sb("sel", [MH, MH, P], F32)
        gbias = sb("gbias", [MH, 2], F32)
        base = place[0]

        def area(offset):
            return [base + offset]

        K = 1024
        a = area(0)
        ya_hi = sb("ya_hi", [P, GG, S], F32R, a)
        ya_lo = sb("ya_lo", [P, GG, S], F32R, a)
        o_hi = sb("o_hi", [P, HH, S], F32R, a)
        o_lo = sb("o_lo", [P, HH, S], F32R, a)
        H_AT = 48 * K
        a = area(H_AT)
        lt = sb("lt", [P, S], F32, a)
        lf = sb("lf", [P, S], F32, a)
        kk = sb("kk", [P, S], F32, a)
        qq = sb("qq", [P, S], F32, a)
        cum = sb("cum", [P, S], F32, a)
        ee = sb("ee", [P, 3, S], F32, a)
        qk = sb("qk", [P, len(LEVELS), S], F32, a)
        sd = sb("sd", [P, NT, P], F32, a)
        so = sb("so", [P, 768], F32, a)
        vT = sb("vT", [P, NT, P], F32, a)
        vf, on = hf[:, 1, :], hf[:, 0, :]
        zo, hsq = sq[:, 1, :], sq[:, 0, :]
        hrs = rstd[:]
        off = sb("off", [P, 3, NCH], F32, a)
        end_h = a[0]
        a = area(16 * K)
        gv = sb("gv", [P, GG, S], F32, a)
        gu = sb("gu", [P, GG, S], F32, a)
        vn = sb("vn", [P, NT, S], F32, a)
        lng = sb("lng", [P, S], F32, a)
        lnb = sb("lnb", [P, S], F32, a)
        bsb = sb("bsb", [P, GG, P], F32, a)
        ws = sb("ws", [P, GG, P], F32, a)
        wsT = sb("wsT", [P, GG, P], F32, a)
        yg = sb("yg", [P, 2, S], F32, a)
        bn = sb("bn", [P, NT, 8], F32, a)
        xtok = sb("xtok", [P, NT, D], F32, a)
        sheets = sb("sheets", [P, 3, P], F32, a)
        maskf = sb("maskf", [P, NMASK, P], F32, a)
        end_g = a[0]
        a = area(H_AT)
        mix_hi = sb("mix_hi", [P, DT, S], F32R, a)
        mix_lo = sb("mix_lo", [P, DT, S], F32R, a)
        sg = sb("sg", [P, 2, S], F32, a)
        gated = sb("gated", [P, 2, S], F32, a)
        end_u = a[0]
        a = area(0)
        f_hi = sb("f_hi", [P, DT, S], F32R, a)
        f_lo = sb("f_lo", [P, DT, S], F32R, a)
        fr = sb("fr", [P, 2, S], F32, a)
        ff = sb("ff", [P, 2, S], F32, a)
        PAD = 4
        a = area(0)
        xm = sb("xm", [P, MT, PAD + S], F32, a)
        xm_hi = sb("xm_hi", [P, MT, S], F32R, a)
        xm_lo = sb("xm_lo", [P, MT, S], F32R, a)
        xc = sb("xc", [P, MT, S], F32, a)
        xc_hi = sb("xc_hi", [P, MT, S], F32R, a)
        xc_lo = sb("xc_lo", [P, MT, S], F32R, a)
        mq = sb("mq", [P, MQ, S], F32, a)
        mk = sb("mk", [P, MQ, S], F32, a)
        mv = sb("mv", [P, NT, S], F32, a)
        st = sb("st", [P, 1280], F32, a)
        ww = sb("ww", [P, 2, S], F32, a)
        og = sb("og", [P, MT, S], F32, a)
        zs = sb("zs", [P, MT, S], F32, a)
        enm, den, nr = hf[:, 1, :], hf[:, 0, :], sq[:, 0, :]
        mpar = sb("mpar", [P, 4 + 3, MT], F32, a)
        bcur = sb("bcur", [P, NT], F32, a)
        bcol = sb("bcol", [P, NT, MH], F32, a)
        wg = sb("wg", [P, DT, 8], F32, a)
        wg_hi = sb("wg_hi", [P, DT, 8], F32R, a)
        wg_lo = sb("wg_lo", [P, DT, 8], F32R, a)
        sel_cur = sb("sel_cur", [MH, P], F32, a)
        rneg = keep[0:MH, :]
        mst = sb("mst", [MH, S], F32, [mask4_at])
        end_m = a[0]
        a = area(9 * K)
        g8 = sb("g8", [8, S], F32, a)
        gi = sb("gi", [MH, S], F32, a)
        gf = sb("gf", [MH, S], F32, a)
        gt = sb("gt", [MH, S], F32, a)
        gF = sb("gF", [MH, S], F32, a)
        gb = sb("gb", [MH, S], F32, a)
        gr = sb("gr", [MH, S], F32, a)
        gone = sb("gone", [MH, S], F32, a)
        a = area(0)
        xr = sb("xr", [P, RT, PAD + S], F32, a)
        rc = sb("rc", [P, RT, S], F32, a)
        rc_hi = sb("rc_hi", [P, RT, S], F32R, a)
        rc_lo = sb("rc_lo", [P, RT, S], F32R, a)
        gw = sb("gw", [P, 2, 7, P], F32, a)
        gw_hi = sb("gw_hi", [P, 2, 7, P], F32R, a)
        gw_lo = sb("gw_lo", [P, 2, 7, P], F32R, a)
        rr = sb("rr", [P, RT, S], F32, a)
        ri = sb("ri", [P, RT, S], F32, a)
        ra = rr
        rt = sb("rt", [P, RT, S], F32, a)
        rh = sb("rh", [P, RT, S], F32, a)
        rg = sb("rg", [P, RT, S], F32, a)
        y_hi = sb("y_hi", [P, RT, S], F32R, a)
        y_lo = sb("y_lo", [P, RT, S], F32R, a)
        ru = hf
        c8 = sb("c8", [P, 2, 12], F32, a)
        ctmp = sb("ctmp", [P, 12], F32, a)
        end_r = a[0]
        a = area(0)
        yf = sb("yf", [P, DT, S], F32, a)
        ytok = sb("ytok", [P, NT, D], F32, a)
        assert max(end_h, end_g, end_u, end_m, end_r) <= nc.sbuf_usable_end, (
            [x - nc.sbuf_usable_end for x in (end_h, end_g, end_u, end_m, end_r)])

        bank = [ctx.enter_context(nc.psum_tensor(f"bank{b}", [P, S], F32)) for b in range(8)]

        raw_full = [sem(f"raw_full{s}") for s in range(RING)]
        hi_ready = [sem(f"hi_ready{s}") for s in range(RING)]
        lo_ready = [sem(f"lo_ready{s}") for s in range(RING)]
        panel_done = [sem(f"panel_done{s}") for s in range(RING)]
        taken = [sem(f"taken{b}") for b in range(RING)]
        aux_free = {b: sem(f"aux_free{b}") for b in (4, 5, 6, 7)}
        raw_zero = sem("raw_zero")
        sp_turn = sem("sp_turn")
        mask_turn = sem("mask_turn")
        x_loaded = sem("x_loaded")
        rows_loaded = sem("rows_loaded")
        g_loaded = sem("g_loaded")
        consts = sem("consts")
        eps_made = sem("eps_made")
        turned = sem("turned")
        x_made = sem("x_made")
        x_normed = sem("x_normed")
        cols_made = sem("cols_made")
        sq_made = sem("sq_made")
        sq_used = sem("sq_used")
        ss_done = sem("ss_done")
        rstd_made = sem("rstd_made")
        hf_made = sem("hf_made")
        hi_made = sem("hi_made")
        h_made = sem("h_made")
        pool_steps = sem("pool_steps")
        act_steps = sem("act_steps")
        dve_steps = sem("dve_steps")
        gv_turned = sem("gv_turned")
        var_made = sem("var_made")
        rs_made = sem("rs_made")
        vn_made = sem("vn_made")
        mixed = sem("mixed")
        yg_made = sem("yg_made")
        yg_hi = sem("yg_hi")
        ya_made = sem("ya_made")
        soft_made = sem("soft_made")
        k_made = sem("k_made")
        expo_made = sem("expo_made")
        decay_made = sem("decay_made")
        qk_made = sem("qk_made")
        v_turned = sem("v_turned")
        level_done = sem("level_done")
        off_done = sem("off_done")
        so_made = sem("so_made")
        av_done = sem("av_done")
        hsq_made = sem("hsq_made")
        hss_done = sem("hss_done")
        hrs_made = sem("hrs_made")
        on_made = sem("on_made")
        ohi_made = sem("ohi_made")
        olo_made = sem("olo_made")
        sig_made = sem("sig_made")
        mixf_made = sem("mixf_made")
        mixhi_made = sem("mixhi_made")
        mix_made = sem("mix_made")
        fr_made = sem("fr_made")
        ff_made = sem("ff_made")
        fhi_made = sem("fhi_made")
        f_made = sem("f_made")
        gates_loaded = sem("gates_loaded")
        gates_hi = sem("gates_hi")
        gates_split = sem("gates_split")
        gates_done = sem("gates_done")
        g8_made = sem("g8_made")
        gf_done = sem("gf_done")
        gpre_made = sem("gpre_made")
        gsoft_made = sem("gsoft_made")
        gb_made = sem("gb_made")
        b_turned = sem("b_turned")
        bcol_made = sem("bcol_made")
        head_set = sem("head_set")
        m_cast = sem("m_cast")
        enm_made = sem("enm_made")
        r_cast = sem("r_cast")
        arg_made = sem("arg_made")
        w_made = sem("w_made")
        xmhi_made = sem("xmhi_made")
        xm_made = sem("xm_made")
        conv_made = sem("conv_made")
        xc_made = sem("xc_made")
        xchi_made = sem("xchi_made")
        xcs_made = sem("xcs_made")
        scores_done = sem("scores_done")
        st_made = sem("st_made")
        den_done = sem("den_done")
        num_done = sem("num_done")
        absden_made = sem("absden_made")
        hh_made = sem("hh_made")
        mean_done = sem("mean_done")
        hc_made = sem("hc_made")
        msq_made = sem("msq_made")
        var_done = sem("var_done")
        mrs_made = sem("mrs_made")
        y_made = sem("y_made")
        yhi_made = sem("yhi_made")
        ys_made = sem("ys_made")
        c8_made = sem("c8_made")
        gw_zero = sem("gw_zero")
        gw_loaded = sem("gw_loaded")
        gw_hi_made = sem("gw_hi_made")
        gw_split = sem("gw_split")
        gw_used = sem("gw_used")
        rchi_made = sem("rchi_made")
        rcs_made = sem("rcs_made")
        ra_made = sem("ra_made")
        rroot_in = sem("rroot_in")
        rroot = sem("rroot")
        ry_made = sem("ry_made")
        ryhi_made = sem("ryhi_made")
        rys_made = sem("rys_made")
        yf_made = sem("yf_made")
        y_turned = sem("y_turned")
        ytok_act = sem("ytok_act")
        ytok_dve = sem("ytok_dve")
        stored = sem("stored")

        block = ctx.enter_context(nc.Block())

        def panel_loaded(eng, p, i=0, per=0):
            eng.wait_ge(raw_full[p % RING], 16 * (p // RING + 1) + i * (16 * (per // RING)))

        def panel_split(eng, p, i=0, per=0):
            eng.wait_ge(lo_ready[p % RING], p // RING + 1 + i * (per // RING))

        def tile_full(eng, p, i=0, per=0):
            eng.wait_ge(panel_done[p % RING], p // RING + 1 + i * (per // RING))

        def tile_taken(eng, t, i=0, per=0):
            eng.wait_ge(taken[t % RING], t // RING + 1 + i * (per // RING))

        def aux_released(eng, b, n, i=0, per=0):
            if not isinstance(i, int) or n + i * per > 0:
                eng.wait_ge(aux_free[b], n + i * per)

        def col(name, j, n=P):
            sheet, at, _ = ROWS[name]
            return cols[0:n, sheet, at + j:at + j + 1]

        @block.sync
        def _(sp):
            x = A["x"][0]
            for n in range(NT):
                sp.dma_start(xtok[:, n, :], x[n * P:(n + 1) * P, :]).then_inc(x_loaded, 16)
            for name, (sheet, at, n) in ROWS.items():
                src = A[name]
                while len(src.shape) > 1:
                    src = src.rearrange("a b -> (a b)") if len(src.shape) == 2 else src.rearrange("a b c -> (a b) c")
                sp.dma_start(sheets[at:at + n, sheet, :], src.rearrange("(r c) -> r c", c=P)).then_inc(rows_loaded, 16)

            def load(p, src, kt, width, i=0, per=0):
                if p >= RING:
                    sp.wait_ge(lo_ready[p % RING], p // RING + i * (per // RING))
                    sp.sem_inc(sp_turn, 1)
                dst = raw[:, p % RING, 0:kt * width].rearrange("p (k c) -> p k c", c=width)
                sp.dma_start(dst, src.rearrange("(k p) c -> p k c", p=P)).then_inc(raw_full[p % RING], 16)

            w_in = A["w_in"][0]
            sp.wait_ge(raw_zero, 1)
            for j in range(GG):
                load(G_P + j, w_in[:, 512 + j * P:512 + (j + 1) * P], 8, P)
            sp.dma_start(ws[:], A["gmlp_ws"][0].rearrange("g q p -> q g p")).then_inc(g_loaded, 16)
            sp.dma_start(lng[:], A["gmlp_ln_g"].to_broadcast([P, S])).then_inc(g_loaded, 16)
            sp.dma_start(lnb[:], A["gmlp_ln_b"].to_broadcast([P, S])).then_inc(g_loaded, 16)
            sp.dma_start(bsb[:].rearrange("p g q -> p (g q)"),
                         A["gmlp_bs"].rearrange("a g q -> a (g q)").to_broadcast([P, S])).then_inc(g_loaded, 16)
            for j in range(GG):
                load(G_P + 4 + j, w_in[:, j * P:(j + 1) * P], 8, P)
            with sp.Fori(0, HH) as i:
                for n, sect in enumerate([2048, 1024, 3072, 4096]):
                    load(H_P + n, w_in[:, bass.ds(i * P + sect, P)], 8, P, i, H_N)
            up_a, up_b = A["w_up_a"][0], A["w_up_b"][0]
            with sp.Fori(0, DT // 2) as i:
                for e in range(2):
                    load(U_P + 4 * e, w_in[:, bass.ds(i * (2 * P) + (5120 + e * P), P)], 8, P, i, U_N)
                    load(U_P + 4 * e + 1, up_a[:, bass.ds(i * (2 * P) + e * P, P)], 4, P, i, U_N)
                    load(U_P + 4 * e + 2, w_in[:, bass.ds(i * (2 * P) + (6144 + e * P), P)], 8, P, i, U_N)
                    load(U_P + 4 * e + 3, up_b[:, bass.ds(i * (2 * P) + e * P, P)], 8, P, i, U_N)
            with sp.Fori(0, 2) as i:
                for e in range(4):
                    load(O_P + e, A["w_out"][0][:, bass.ds(i * (4 * P) + e * P, P)], 8, P, i, 4)
            with sp.Fori(0, 4) as i:
                for e in range(8):
                    load(F_P + e, A["w_ff1"][0][:, bass.ds(i * D + e * P, P)], 8, P, i, F_N)
                for e in range(8):
                    load(F_P + 8 + e, A["w_ff2"][0][bass.ds(i * D, D), e * P:(e + 1) * P], 8, P, i, F_N)
            tile_taken(sp, F_T + F_N - 1)
            m_in = A["m_w_in_2"][0]
            sp.dma_start(wg[:], m_in[:, 6144:6152].rearrange("(k p) c -> p k c", p=P)).then_inc(gates_loaded, 16)
            sp.dma_start(gbias[:, 0:1], A["m_b_i_2"].rearrange("a h -> h a")).then_inc(gates_loaded, 16)
            sp.dma_start(gbias[:, 1:2], A["m_b_f_2"].rearrange("a h -> h a")).then_inc(gates_loaded, 16)
            with sp.Fori(0, MH) as i:
                for e in range(4):
                    load(M_P + e, m_in[:, bass.ds(i * S + e * P, P)], 8, P, i, M_NP)
                for e in range(4):
                    load(M_P + 4 + e, m_in[:, bass.ds(i * S + (4096 + e * P), P)], 8, P, i, M_NP)
                flat = [A[n][0].rearrange("h r c -> (h r) c") for n in ("m_w_q_2", "m_w_k_2", "m_w_v_2")]
                load(M_P + 8, flat[0][bass.ds(i * S, S), :], 4, 2 * P, i, M_NP)
                load(M_P + 9, flat[1][bass.ds(i * S, S), :], 4, 2 * P, i, M_NP)
                for e in range(2):
                    load(M_P + 10 + e, flat[2][bass.ds(i * S, S), e * 2 * P:(e + 1) * 2 * P], 4, 2 * P, i, M_NP)
                for e in range(4):
                    load(M_P + 12 + e, m_in[:, bass.ds(i * S + (2048 + e * P), P)], 8, P, i, M_NP)
                for e in range(4):
                    load(M_P + 16 + e, A["m_w_out_2"][0][bass.ds(i * S, S), e * 2 * P:(e + 1) * 2 * P],
                         4, 2 * P, i, M_NP)
            r_in, r_out = A["r_w_in_2"][0], A["r_w_out_2"][0]
            for i in range(RG):
                p0 = R_P + i * R_NP
                for e in range(RT):
                    load(p0 + e, r_in[:, (i * RT + e) * P:(i * RT + e + 1) * P], 8, P)
                if i == 0:
                    sp.wait_ge(gw_zero, 1)
                else:
                    sp.wait_ge(gw_split, 2 * i)
                for z, name in enumerate(("r_w_a_2", "r_w_x_2")):
                    w = A[name][0, 2 * i]
                    sp.dma_start(gw[:, z, 0, :], w[0:P, 0:P]).then_inc(gw_loaded, 16)
                    sp.dma_start(gw[0:64, z, 1, :], w[P:192, 0:P]).then_inc(gw_loaded, 16)
                    sp.dma_start(gw[:, z, 2, 0:64], w[0:P, P:192]).then_inc(gw_loaded, 16)
                    sp.dma_start(gw[0:64, z, 3, 0:64], w[P:192, P:192]).then_inc(gw_loaded, 16)
                    w = A[name][0, 2 * i + 1]
                    sp.dma_start(gw[64:P, z, 3, 64:P], w[0:64, 0:64]).then_inc(gw_loaded, 16)
                    sp.dma_start(gw[:, z, 4, 64:P], w[64:192, 0:64]).then_inc(gw_loaded, 16)
                    sp.dma_start(gw[64:P, z, 5, :], w[0:64, 64:192]).then_inc(gw_loaded, 16)
                    sp.dma_start(gw[:, z, 6, :], w[64:192, 64:192]).then_inc(gw_loaded, 16)
                for e in range(RT):
                    load(p0 + 3 + e, r_in[:, RW + (i * RT + e) * P:RW + (i * RT + e + 1) * P], 8, P)
                for e in range(4):
                    load(p0 + 6 + e, r_out[i * RT * P:(i + 1) * RT * P, e * 2 * P:(e + 1) * 2 * P], RT, 2 * P)
            for n in range(NT):
                sp.wait_ge(ytok_act, n + 1)
                sp.wait_ge(ytok_dve, n + 1)
                sp.dma_start(out[0, n * P:(n + 1) * P, :], ytok[:, n, :]).then_inc(stored, 16)
            sp.wait_ge(stored, 16 * NT)

        @block.gpsimd
        def _(pool):
            steps = Steps(pool, pool_steps)
            pool.memset(raw[:], 0.0).then_inc(raw_zero, 1)
            pool.memset(ones[:], 1.0)
            pool.memset(ones_m[:], 1.0 / S)
            steps.link(pool.memset(keep[:], 1.0))
            steps.link(pool.memset(keep[:].rearrange("p (c s) -> p c s", s=CHUNK)[:, :, 0:1], 0.0))
            steps.link(pool.memset(ident[:], 0.0))
            steps.link(pool.affine_select(out=ident[:], in_=ident[:], compare_op=ALU.not_equal, fill=1.0, base=0,
                                          pattern=[[-1, P]], channel_multiplier=1))
            steps.link(pool.memset(cap[:], 0.0))
            steps.link(pool.affine_select(out=cap[:], in_=cap[:], compare_op=ALU.is_ge, fill=-1e30, base=0,
                                          pattern=[[1, P]], channel_multiplier=-1))
            steps.link(pool.memset(maskf[:], 0.0))
            pool.tensor_copy(maskf[:, 0, :], ident[:])
            for m in range(1, NMASK):
                h = LEVELS[m - 1]
                nb = P // (2 * h)
                pairs = maskf[:, m, 0:P // 2].rearrange("p (b t) -> p b t", t=h)
                steps.link(pool.memset(pairs, 1.0))
                steps.link(pool.affine_select(out=pairs, in_=pairs, compare_op=ALU.is_ge, fill=0.0, base=0,
                                              pattern=[[-2 * h, nb], [0, h]], channel_multiplier=1))
                steps.link(pool.affine_select(out=pairs, in_=pairs, compare_op=ALU.is_ge, fill=0.0, base=h - 1,
                                              pattern=[[2 * h, nb], [0, h]], channel_multiplier=-1))
            steps.link(pool.memset(sel[:], 0.0))
            pool.affine_select(out=sel[:], in_=sel[:], compare_op=ALU.not_equal, fill=1.0, base=0,
                               pattern=[[-1, MH], [0, P]], channel_multiplier=1).then_inc(consts, 1)
            with pool.Fori(0, N_PANELS // RING) as i:
                for s in range(RING):
                    pool.wait_ge(hi_ready[s], i + 1)
                    pool.tensor_tensor(w_lo[:, s, :], raw[:, s, :], w_hi[:, s, :].bitcast(F32),
                                       ALU.subtract).then_inc(lo_ready[s], 1)

        @block.tensor
        def _(pe):
            def products(p, outs, hi, lo, kt, i=0, per=0, need=None):
                panel_split(pe, p, i, per)
                for o, dst in enumerate(outs):
                    for k in range(kt):
                        if need and o == 0:
                            need(k)
                        c = (k * len(outs) + o) * P
                        wh, wl = w_hi[:, p % RING, c:c + P], w_lo[:, p % RING, c:c + P]
                        pe.matmul(dst, wh, hi[:, k, :], start=(k == 0), stop=False)
                        pe.matmul(dst, wh, lo[:, k, :], start=False, stop=False)
                        mm = pe.matmul(dst, wl, hi[:, k, :], start=False, stop=(k == kt - 1))
                mm.then_inc(panel_done[p % RING], 1)

            def bank_ready(t, i=0, per=0):
                if t >= RING:
                    pe.wait_ge(taken[t % RING], t // RING + i * (per // RING))

            def dense(p, t, i=0, per=0, per_t=None, hi=h_hi, lo=h_lo, kt=8, need=None, width=1):
                for e in range(width):
                    bank_ready(t + e, i, per if per_t is None else per_t)
                products(p, [bank[(t + e) % RING][:] for e in range(width)], hi, lo, kt, i, per, need)

            def norm_sums(n):
                aux_released(pe, 4, NORM_AUX[n])
                for j in range(DT):
                    pe.wait_ge(sq_made, DT * n + j + 1)
                    pe.matmul(bank[4][:], ones[:], sq[:, j % 2, :], start=(j == 0),
                              stop=(j == DT - 1)).then_inc(sq_used, 1)

            def normed(n):
                return lambda k: pe.wait_ge(h_made, DT * n + k + 1)

            pe.wait_ge(consts, 1)
            pe.wait_ge(rows_loaded, 16 * len(ROWS))
            for s in range(3):
                n = SHEET_ROWS[s]
                pe.transpose(bank[4 + s][:, 0:n], sheets[0:n, s, :], ident[0:n, 0:n]).then_inc(turned, 1)
            pe.wait_ge(g_loaded, 64)
            for g in range(GG):
                mm = pe.transpose(bank[7][:, g * P:(g + 1) * P], ws[:, g, :], ident[:])
            mm.then_inc(turned, 1)
            pe.wait_ge(x_loaded, 16 * NT)
            for j in range(DT):
                aux_released(pe, 4 + j % 4, 1 + j // 4)
                for n in range(NT):
                    mm = pe.transpose(bank[4 + j % 4][:, n * P:(n + 1) * P], xtok[:, n, j * P:(j + 1) * P], ident[:])
                mm.then_inc(turned, 1)
            norm_sums(0)

            for j in range(GG):
                dense(G_P + j, G_T + j, need=normed(0) if j == 0 else None)
            dense(G_P + 4, G_T + 4)
            for n in range(NT):
                aux_released(pe, 4 + n, AUX_G[4 + n])
                for g in range(GG):
                    if n == 0:
                        tile_taken(pe, G_T + g)
                    mm = pe.transpose(bank[4 + n][:, g * P:(g + 1) * P], gv[:, g, n * P:(n + 1) * P], ident[:])
                mm.then_inc(gv_turned, 1)
            for j in range(1, GG):
                dense(G_P + 4 + j, G_T + 4 + j)
            for g in range(GG):
                aux_released(pe, 4 + g, AUX_G[4 + g] + 1)
                for n in range(NT):
                    if g == 0:
                        pe.wait_ge(vn_made, n + 1)
                    mm = pe.matmul(bank[4 + g][:, n * P:(n + 1) * P], vn[:, n, g * P:(g + 1) * P], wsT[:, g, :],
                                   start=True, stop=True, skip_group_check=True)
                mm.then_inc(mixed, 1)

            def head_in(i, half):
                for e in (0, 1):
                    dense(H_P + 2 * half + e, H_T + 2 * half + e, i, H_N)

            def head_scores(i):
                def free(b, n):
                    aux_released(pe, b, AUX_H[b] + n, i, H_AUX[b])
                free(7, 0)
                tile_taken(pe, H_T + 2, i, H_N)
                for n in range(NT):
                    mm = pe.transpose(bank[7][:, n * P:(n + 1) * P], vf[:, n * P:(n + 1) * P], ident[:])
                mm.then_inc(v_turned, 1)
                for m in range(NMASK):
                    b, at = M_BANK[m], M_AT[m]
                    if at == 0:
                        free(b, {0: 0, 7: 1}.get(m, 1 if b == 7 else 0))
                    if m == 0:
                        pe.wait_ge(k_made, i + 1)
                        tile_taken(pe, H_T + 1, i, H_N)
                    else:
                        pe.wait_ge(qk_made, i * len(LEVELS) + m)
                    for n in range(NT):
                        c = slice(n * P, (n + 1) * P)
                        if m == 0:
                            mm = pe.matmul(bank[b][:, c], kk[:, c], qq[:, c], start=True, stop=True,
                                           skip_group_check=True)
                        else:
                            h = LEVELS[m - 1]
                            right = qk[:, m - 1, c].rearrange("p (b two t) -> p b two t", two=2, t=h)[:, :, 1, :]
                            dst = bank[b][:, at + n * 64:at + n * 64 + 64].rearrange("p (b t) -> p b t", t=h)
                            mm = pe.matmul(dst, qk[:, m - 1, c], right, start=True, stop=True,
                                           skip_group_check=True)
                    mm.then_inc(level_done, 1)
                free(4, 2)
                free(5, 1)
                pe.wait_ge(qk_made, i * len(LEVELS) + len(LEVELS))
                q128, q256 = qk[:, 7, :], qk[:, 8, :]
                for dst, src, s0, t0, t1 in ((bank[4][:, 0:128], q128, 0, 128, 256),
                                             (bank[4][:, 384:512], q128, 256, 384, 512),
                                             (bank[4][:, 128:384], q256, 0, 256, 512),
                                             (bank[5][:, 0:256], q256, 128, 256, 512)):
                    mm = pe.matmul(dst, src[:, s0:s0 + P], src[:, t0:t1], start=True, stop=True,
                                   skip_group_check=True)
                mm.then_inc(off_done, 1)

            def head_values(i):
                aux_released(pe, 6, AUX_H[6] + 1, i, H_AUX[6])
                aux_released(pe, 7, AUX_H[7] + 2, i, H_AUX[7])
                pe.wait_ge(so_made, i + 1)
                o = bank[6]
                pe.matmul(o[:, 128:512], vT[:, 0, :], so[:, 0:384], start=True, stop=False, skip_group_check=True)
                pe.matmul(o[:, 0:128], vT[:, 0, :], sd[:, 0, :], start=False, stop=False, skip_group_check=True)
                pe.matmul(o[:, 256:512], vT[:, 1, :], so[:, 512:768], start=False, stop=False, skip_group_check=True)
                pe.matmul(o[:, 128:256], vT[:, 1, :], sd[:, 1, :], start=False, stop=False, skip_group_check=True)
                pe.matmul(o[:, 384:512], vT[:, 2, :], so[:, 384:512], start=False, stop=False, skip_group_check=True)
                pe.matmul(o[:, 256:384], vT[:, 2, :], sd[:, 2, :], start=False, stop=False, skip_group_check=True)
                pe.matmul(o[:, 384:512], vT[:, 3, :], sd[:, 3, :], start=False, stop=True,
                          skip_group_check=True).then_inc(av_done, 1)
                pe.wait_ge(hsq_made, i + 1)
                pe.matmul(bank[7][:], ones[:], hsq, start=True, stop=True).then_inc(hss_done, 1)

            head_in(0, 0)
            head_in(0, 1)
            with pe.Fori(0, HH - 1) as i:
                head_in(i + 1, 0)
                head_scores(i)
                head_in(i + 1, 1)
                head_values(i)
            head_scores(HH - 1)
            head_values(HH - 1)

            def ups(i, need_a=None, need_b=None):
                for e in range(2):
                    dense(U_P + 4 * e, U_T + 4 * e, i, U_N)
                    pe.wait_ge(ya_made, GG)
                    dense(U_P + 4 * e + 1, U_T + 4 * e + 1, i, U_N, hi=ya_hi, lo=ya_lo, kt=4)
                    dense(U_P + 4 * e + 2, U_T + 4 * e + 2, i, U_N)
                    pe.wait_ge(olo_made, HH)
                    dense(U_P + 4 * e + 3, U_T + 4 * e + 3, i, U_N, hi=o_hi, lo=o_lo)
            with pe.Fori(0, DT // 2) as i:
                ups(i)
            for j in range(DT):
                dense(O_P + j, O_T + j, hi=mix_hi, lo=mix_lo,
                      need=(lambda k: pe.wait_ge(mix_made, k + 2)) if j == 0 else None)

            norm_sums(1)

            def ffn(i):
                for e in range(8):
                    if e == 0:
                        pe.wait_ge(h_made, 2 * DT)
                    dense(F_P + e, F_T + e, i, F_N)
                for e in range(8):
                    dense(F_P + 8 + e, F_T + 8 + e, i, F_N, hi=f_hi, lo=f_lo,
                          need=(lambda k: pe.wait_ge(f_made, i * DT + (k + 1))) if e == 0 else None)
            with pe.Fori(0, 4) as i:
                ffn(i)

            norm_sums(2)
            norm_sums(3)
            pe.wait_ge(gates_split, 1)
            for k in range(DT):
                pe.wait_ge(h_made, 2 * DT + k + 1)
                pe.matmul(bank[5][0:8, :], wg_hi[:, k, :], h_hi[:, k, :], start=(k == 0), stop=False)
                pe.matmul(bank[5][0:8, :], wg_hi[:, k, :], h_lo[:, k, :], start=False, stop=False)
                mm = pe.matmul(bank[5][0:8, :], wg_lo[:, k, :], h_hi[:, k, :], start=False, stop=(k == DT - 1))
            mm.then_inc(gates_done, 1)
            pe.wait_ge(g8_made, 1)
            pe.matmul(bank[6][0:MH, :], ident[0:8, 4:8], g8[:], start=True, stop=True).then_inc(gf_done, 1)
            pe.wait_ge(gb_made, 1)
            for n in range(NT):
                mm = pe.transpose(bank[7][:, n * MH:(n + 1) * MH], gb[:, n * P:(n + 1) * P], ident[0:MH, 0:MH])
            mm.then_inc(b_turned, 1)

            spans = [(0, 0, 4), (512, 1, 5), (896, 2, 6), (1152, 3, 6)]

            def score_bank(n):
                return bank[[4, 5, 6, 6][n]], [0, 0, 0, 256][n]

            def mlstm(i):
                def free(b, n):
                    aux_released(pe, b, AUX_M[b] + n, i, 2)
                pe.wait_ge(head_set, i + 1)
                free(7, 0)
                pe.matmul(bank[7][:], sel_cur[:], mst[:], start=True, stop=True).then_inc(m_cast, 1)
                free(7, 1)
                pe.matmul(bank[7][:], sel_cur[:], rneg, start=True, stop=True).then_inc(r_cast, 1)
                for e in range(8):
                    dense(M_P + e, M_T + e, i, M_NP, M_NT)
                for z in range(2):
                    dense(M_P + 8 + z, M_T + 8 + 2 * z, i, M_NP, M_NT, hi=xc_hi, lo=xc_lo, kt=4, width=2,
                          need=(lambda k: pe.wait_ge(xcs_made, i * MT + (k + 1))) if z == 0 else None)
                for z in range(2):
                    p = M_P + 10 + z
                    panel_split(pe, p, i, M_NP)
                    if z == 0:
                        pe.wait_ge(xm_made, (i + 1) * MT)
                    for n in range(NT):
                        if z == 0:
                            bank_ready(M_T + 12 + n, i, M_NT)
                        dst = bank[(M_T + 12 + n) % RING][:, z * 256:(z + 1) * 256]
                        c = slice(n * P, (n + 1) * P)
                        for k in range(MT):
                            wh = w_hi[:, p % RING, k * 256:(k + 1) * 256]
                            wl = w_lo[:, p % RING, k * 256:(k + 1) * 256]
                            pe.matmul(dst, xm_hi[:, k, c], wh, start=(k == 0), stop=False, skip_group_check=True)
                            pe.matmul(dst, xm_hi[:, k, c], wl, start=False, stop=False, skip_group_check=True)
                            mm = pe.matmul(dst, xm_lo[:, k, c], wh, start=False, stop=(k == MT - 1),
                                           skip_group_check=True)
                    mm.then_inc(panel_done[p % RING], 1)
                    if z == 0:
                        for e in range(MQ):
                            tile_taken(pe, M_T + 8 + e, i, M_NT)
                            tile_taken(pe, M_T + 10 + e, i, M_NT)
                        free(4, 0)
                        free(5, 0)
                        free(6, 0)
                        for n in range(NT):
                            b, at = score_bank(n)
                            width = S - n * P
                            for e in range(MQ):
                                mm = pe.matmul(b[:, at:at + width], mk[:, e, n * P:(n + 1) * P],
                                               mq[:, e, n * P:S], start=(e == 0 and n != 3), stop=(e == MQ - 1),
                                               skip_group_check=True)
                            mm.then_inc(scores_done, 1)
                place_st = [0, 512, 896, 1152]
                free(4, 1)
                for n in range(NT):
                    pe.wait_ge(st_made, i * NT + (n + 1))
                    w = S - n * P
                    mm = pe.matmul(bank[4][:, n * P:S], ones[:], st[:, place_st[n]:place_st[n] + w],
                                   start=(n == 0), stop=(n == NT - 1), skip_group_check=True)
                mm.then_inc(den_done, 1)
                for d in range(MT):
                    t = M_T + 16 + d
                    bank_ready(t, i, M_NT)
                    if d == 0:
                        for n in range(NT):
                            tile_taken(pe, M_T + 12 + n, i, M_NT)
                    for n in range(NT):
                        w = S - n * P
                        mm = pe.matmul(bank[t % RING][:, n * P:S], mv[:, n, d * P:(d + 1) * P],
                                       st[:, place_st[n]:place_st[n] + w], start=(n == 0), stop=(n == NT - 1),
                                       skip_group_check=True)
                    mm.then_inc(num_done, 1)
                dense(M_P + 12, M_T + 20, i, M_NP, M_NT)
                dense(M_P + 13, M_T + 21, i, M_NP, M_NT)
                free(5, 1)
                for d in range(MT):
                    pe.wait_ge(hh_made, i * MT + (d + 1))
                    mm = pe.matmul(bank[5][:], ones_m[:], xm[:, d, PAD:], start=(d == 0), stop=(d == MT - 1))
                mm.then_inc(mean_done, 1)
                dense(M_P + 14, M_T + 22, i, M_NP, M_NT)
                free(6, 1)
                for d in range(MT):
                    pe.wait_ge(msq_made, i * MT + (d + 1))
                    mm = pe.matmul(bank[6][:], ones_m[:], sq[:, d % 2, :], start=(d == 0), stop=(d == MT - 1))
                    mm.then_inc(var_done, 1)
                dense(M_P + 15, M_T + 23, i, M_NP, M_NT)
                for e in range(4):
                    dense(M_P + 16 + e, M_T + 24 + 2 * e, i, M_NP, M_NT, hi=xm_hi, lo=xm_lo, kt=4, width=2,
                          need=(lambda k: pe.wait_ge(ys_made, i * MT + (k + 1))) if e == 0 else None)
            with pe.Fori(0, MH) as i:
                mlstm(i)

            norm_sums(4)
            for i in range(RG):
                p0, t0 = R_P + i * R_NP, R_T + i * R_NT
                for e in range(4):
                    dense(p0 + e, t0 + e, need=normed(3) if i == 0 and e == 0 else None)
                pe.wait_ge(gw_split, 2 * (i + 1))
                pe.wait_ge(rcs_made, RT * (i + 1))
                for z in range(2):
                    for o, blocks in enumerate([[(0, 0), (1, 1)], [(2, 0), (3, 1), (4, 2)], [(5, 1), (6, 2)]]):
                        t = t0 + 4 + z * RT + o
                        bank_ready(t)
                        dst = bank[t % RING][:]
                        for n, (wb, k) in enumerate(blocks):
                            pe.matmul(dst, gw_hi[:, z, wb, :], rc_hi[:, k, :], start=(n == 0), stop=False)
                            pe.matmul(dst, gw_hi[:, z, wb, :], rc_lo[:, k, :], start=False, stop=False)
                            mm = pe.matmul(dst, gw_lo[:, z, wb, :], rc_hi[:, k, :], start=False,
                                           stop=(n == len(blocks) - 1))
                        mm.then_inc(gw_used, 1)
                dense(p0 + 4, t0 + 10)
                dense(p0 + 5, t0 + 11)
                for e in range(4):
                    dense(p0 + 6 + e, t0 + 12 + 2 * e, hi=y_hi, lo=y_lo, kt=RT, width=2,
                          need=(lambda k: pe.wait_ge(rys_made, RT * i + k + 1)) if e == 0 else None)

            norm_sums(5)
            for n in range(NT):
                for half in range(2):
                    u = 2 * n + half
                    b = 4 + u % 4
                    aux_released(pe, b, AUX_E[b] + u // 4)
                    for j in range(4):
                        if n == 0:
                            pe.wait_ge(yf_made, half * 4 + j + 1)
                        mm = pe.transpose(bank[b][:, j * P:(j + 1) * P], yf[:, half * 4 + j, n * P:(n + 1) * P],
                                          ident[:])
                    mm.then_inc(y_turned, 1)

        @block.scalar
        def _(act):
            steps = Steps(act, act_steps)
            link = lambda ins: steps.link(ins)

            def upper(p, i=0, per=0):
                if isinstance(i, int) and p + i * per >= N_PANELS:
                    return
                panel_loaded(act, p, i, per)
                if p >= RING:
                    act.wait_ge(panel_done[p % RING], p // RING + i * (per // RING))
                act.activation(w_hi[:, p % RING, :], raw[:, p % RING, :], ACT.Copy).then_inc(hi_ready[p % RING], 1)

            def square_x(n, ready):
                for j in range(DT):
                    ready(j)
                    if j >= 2 or n:
                        act.wait_ge(sq_used, DT * n + j - 1 if j >= 2 else DT * n)
                    act.activation(sq[:, j % 2, :], xT[:, j, :], ACT.Square).then_inc(sq_made, 1)
                act.wait_ge(sq_used, DT * (n + 1))
                act.activation(rstd[:], bank[4][:], ACT.Ln, bias=eps, scale=1.0 / D).then_inc(aux_free[4], 1)
                act.wait_ge(aux_free[4], NORM_AUX[n] + 1)
                act.activation(rstd[:], rstd[:], ACT.Exp, scale=-0.5).then_inc(rstd_made, 1)

            def norm_upper(n):
                for j in range(DT):
                    act.wait_ge(hf_made, DT * n + j + 1)
                    act.activation(h_hi[:, j, :], hf[:, j % 2, :], ACT.Copy).then_inc(hi_made, 1)

            act.wait_ge(eps_made, 1)
            eps = small[:, 0:1]
            upper(0)
            upper(1)
            upper(2)
            square_x(0, lambda j: act.wait_ge(x_made, j + 1))
            norm_upper(0)
            for j in range(GG):
                upper(G_P + j + 3)
                tile_full(act, G_P + j)
                act.activation(gv[:, j, :], bank[(G_T + j) % RING][:], ACT.Gelu).then_inc(taken[(G_T + j) % RING], 1)
            for j in range(GG):
                upper(G_P + 4 + j + 3)
                tile_full(act, G_P + 4 + j)
                act.activation(gu[:, j, :], bank[(G_T + 4 + j) % RING][:], ACT.Gelu)\
                   .then_inc(taken[(G_T + 4 + j) % RING], 1)
            act.wait_ge(var_made, 1)
            lnv = small[:, 8:12]
            link(act.activation(lnv, bn[:, :, 7], ACT.Ln, bias=eps))
            act.activation(lnv, lnv, ACT.Exp, scale=-0.5).then_inc(rs_made, 1)
            for g in range(GG):
                act.wait_ge(yg_made, g + 1)
                act.activation(ya_hi[:, g, :], yg[:, g % 2, :], ACT.Copy).then_inc(yg_hi, 1)

            def head_soft(i):
                tile_full(act, H_P, i, H_N)
                if not isinstance(i, int) or i > 0:
                    act.wait_ge(level_done, i * NMASK - (NMASK - 1))
                    act.wait_ge(qk_made, i * len(LEVELS))
                tile_full(act, H_P + 1, i, H_N)
                act.activation(qq[:], bank[(H_T + 1) % RING][:], ACT.Silu).then_inc(taken[(H_T + 1) % RING], 1)
                link(act.activation(lt[:], bank[H_T % RING][:], ACT.Abs))
                link(act.activation(lt[:], lt[:], ACT.Exp, scale=-1.0))
                act.activation(lt[:], lt[:], ACT.Ln, bias=1.0).then_inc(soft_made, 1)

            def head_decays(i, before=None):
                tile_taken(act, H_T, i, H_N)
                act.activation(kk[:], kk[:], ACT.Exp).then_inc(k_made, 1)
                for l in range(len(LEVELS)):
                    if l == 3 and before is not None:
                        head_square(before)
                    act.wait_ge(expo_made, i * len(LEVELS) + (l + 1))
                    act.activation(ee[:, l % 3, :], ee[:, l % 3, :], ACT.Exp).then_inc(decay_made, 1)

            def head_v(i):
                tile_full(act, H_P + 2, i, H_N)
                if not isinstance(i, int) or i > 0:
                    act.wait_ge(v_turned, i)
                act.activation(vf, bank[(H_T + 2) % RING][:], ACT.Copy).then_inc(taken[(H_T + 2) % RING], 1)

            def head_z(i):
                tile_full(act, H_P + 3, i, H_N)
                if not isinstance(i, int) or i > 0:
                    act.wait_ge(on_made, i)
                act.activation(zo, bank[(H_T + 3) % RING][:], ACT.Silu).then_inc(taken[(H_T + 3) % RING], 1)

            def head_vT(i):
                act.wait_ge(v_turned, i + 1)
                act.activation(vT[:].rearrange("p n c -> p (n c)"), bank[7][:], ACT.Copy).then_inc(aux_free[7], 1)

            def head_off(i):
                act.wait_ge(off_done, i + 1)
                act.activation(so[:, 0:512], bank[4][:], ACT.Copy).then_inc(aux_free[4], 1)
                act.activation(so[:, 512:768], bank[5][:, 0:256], ACT.Copy).then_inc(aux_free[5], 1)
                act.wait_ge(aux_free[4], AUX_H[4] + 3 + i * H_AUX[4])
                act.wait_ge(aux_free[5], AUX_H[5] + 2 + i * H_AUX[5])
                act.sem_inc(so_made, 1)

            def head_square(i):
                act.wait_ge(av_done, i + 1)
                act.activation(hsq, bank[6][:], ACT.Square).then_inc(hsq_made, 1)

            def head_norm(i):
                act.wait_ge(hss_done, i + 1)
                act.activation(hrs, bank[7][:], ACT.Ln, bias=eps, scale=1.0 / P).then_inc(aux_free[7], 1)
                act.wait_ge(aux_free[7], AUX_H[7] + 3 + i * H_AUX[7])
                act.activation(hrs, hrs, ACT.Exp, scale=-0.5).then_inc(hrs_made, 1)
                act.wait_ge(on_made, i + 1)
                dst = o_hi[:, i, :] if isinstance(i, int) else o_hi[:, bass.ds(i, 1), :].rearrange("p a s -> p (a s)")
                act.activation(dst, on, ACT.Copy).then_inc(ohi_made, 1)

            act.wait_ge(ya_made, GG)
            head_soft(0)
            upper(H_P + 3)
            head_decays(0)
            head_v(0)
            upper(H_P + 4)
            upper(H_P + 5)
            head_z(0)
            upper(H_P + 6)

            def heads(i):
                upper(H_P + 7, i, H_N)
                head_vT(i)
                head_soft(i + 1)
                upper(H_P + 8, i, H_N)
                head_off(i)
                head_v(i + 1)
                upper(H_P + 9, i, H_N)
                head_decays(i + 1, i)
                upper(H_P + 10, i, H_N)
                head_norm(i)
                head_z(i + 1)
            steps.loop(HH - 1, 2, heads)
            last = HH - 1
            upper(U_P + 3)
            head_vT(last)
            head_off(last)
            head_square(last)
            head_norm(last)

            def ups(i):
                for e in range(2):
                    for z in range(2):
                        n = 4 * e + 2 * z
                        tile_full(act, U_P + n, i, U_N)
                        upper(U_P + n + 4, i, U_N)
                        act.activation(sg[:, z, :], bank[(U_T + n) % RING][:], ACT.Sigmoid)\
                           .then_inc(taken[(U_T + n) % RING], 1)
                        tile_full(act, U_P + n + 1, i, U_N)
                        upper(U_P + n + 5, i, U_N)
                    act.wait_ge(mixf_made, i * 2 + (e + 1))
                    j = i * 2 + e
                    act.activation(mix_hi[:, bass.ds(j, 1), :].rearrange("p a s -> p (a s)"), gated[:, 0, :],
                                   ACT.Copy).then_inc(mixhi_made, 1)
            steps.loop(DT // 2, 0, ups)

            for j in range(DT):
                tile_full(act, O_P + j)
                upper(O_P + j + 4)
            square_x(1, lambda j: tile_taken(act, O_T + j))
            norm_upper(1)

            def ffn(i):
                for e in range(8):
                    tile_full(act, F_P + e, i, F_N)
                    upper(F_P + e + 4, i, F_N)
                    c = i * 8 + e
                    if e >= 2:
                        act.wait_ge(ff_made, c - 1)
                    act.activation(fr[:, e % 2, :], bank[(F_T + e) % RING][:], ACT.Relu)\
                       .then_inc(taken[(F_T + e) % RING], 1)
                    act.wait_ge(ff_made, c + 1)
                    act.activation(f_hi[:, e, :], ff[:, e % 2, :], ACT.Copy).then_inc(fhi_made, 1)
                for e in range(8):
                    tile_full(act, F_P + 8 + e, i, F_N)
                    upper(F_P + e + 12, i, F_N)
            steps.loop(4, 0, ffn)

            square_x(2, lambda j: tile_taken(act, F_T + 3 * F_N + 8 + j))
            square_x(3, lambda j: act.wait_ge(x_normed, j + 1))
            act.wait_ge(gates_loaded, 48)
            act.activation(wg_hi[:].rearrange("p k c -> p (k c)"), wg[:].rearrange("p k c -> p (k c)"),
                           ACT.Copy).then_inc(gates_hi, 1)
            norm_upper(2)
            act.wait_ge(gates_done, 1)
            act.activation(g8[:], bank[5][0:8, :], ACT.Copy).then_inc(aux_free[5], 1)
            act.wait_ge(aux_free[5], AUX_MP[5] + 1)
            act.sem_inc(g8_made, 1)
            link(act.activation(gi[:], g8[0:MH, :], ACT.Identity, bias=gbias[:, 0:1]))
            act.wait_ge(gf_done, 1)
            act.activation(gf[:], bank[6][0:MH, :], ACT.Identity, bias=gbias[:, 1:2]).then_inc(aux_free[6], 1)
            act.wait_ge(aux_free[6], AUX_MP[6] + 1)
            link(act.activation(gt[:], gf[:], ACT.Abs))
            link(act.activation(gt[:], gt[:], ACT.Exp, scale=-1.0))
            act.activation(gt[:], gt[:], ACT.Ln, bias=1.0).then_inc(gsoft_made, 1)

            def mlstm(i):
                act.wait_ge(m_cast, i + 1)
                act.activation(enm, bank[7][:], ACT.Exp, scale=-1.0).then_inc(aux_free[7], 1)
                act.wait_ge(r_cast, i + 1)
                act.activation(nr, bank[7][:], ACT.Copy).then_inc(aux_free[7], 1)
                for c in range(MT):
                    tile_full(act, M_P + c, i, M_NP)
                    upper(M_P + c + 4, i, M_NP)
                    if c == 0:
                        tile_full(act, M_P - 1, i, M_NP)
                    link(act.activation(xm[:, c, PAD:], bank[(M_T + c) % RING][:], ACT.Copy))
                    act.activation(xm_hi[:, c, :], xm[:, c, PAD:], ACT.Copy).then_inc(xmhi_made, 1)
                    if c >= 1:
                        conv_out(i, c - 1)
                conv_out(i, MT - 1)
                for c in range(MT):
                    tile_full(act, M_P + 4 + c, i, M_NP)
                    upper(M_P + c + 8, i, M_NP)
                    act.activation(og[:, c, :], bank[(M_T + 4 + c) % RING][:], ACT.Sigmoid)\
                       .then_inc(taken[(M_T + 4 + c) % RING], 1)
                for z, dst in ((0, mq), (1, mk)):
                    tile_full(act, M_P + 8 + z, i, M_NP)
                    upper(M_P + 12 + z, i, M_NP)
                    for e in range(MQ):
                        t = M_T + 8 + 2 * z + e
                        act.activation(dst[:, e, :], bank[t % RING][:], ACT.Copy,
                                       scale=1.0 / 16 if z == 0 else 1.0).then_inc(taken[t % RING], 1)
                for n in range(NT):
                    if n >= 2:
                        act.wait_ge(st_made, i * NT + (n - 1))
                    act.wait_ge(arg_made, i * NT + (n + 1))
                    link(act.activation(ww[:, n % 2, n * P:(n + 1) * P], ww[:, n % 2, n * P:(n + 1) * P], ACT.Exp))
                    if n < NT - 1:
                        act.activation(ww[:, n % 2, (n + 1) * P:S], nr[:, (n + 1) * P:S], ACT.Exp,
                                       bias=bcur[:, n:n + 1]).then_inc(w_made, 1)
                    else:
                        act.sem_inc(w_made, 1)
                tile_full(act, M_P + 10, i, M_NP)
                upper(M_P + 14, i, M_NP)
                tile_full(act, M_P + 11, i, M_NP)
                upper(M_P + 15, i, M_NP)
                for n in range(NT):
                    t = M_T + 12 + n
                    act.activation(mv[:, n, :], bank[t % RING][:], ACT.Copy).then_inc(taken[t % RING], 1)
                act.wait_ge(den_done, i + 1)
                act.activation(den, bank[4][:], ACT.Abs).then_inc(aux_free[4], 1)
                for c in range(MT):
                    tile_full(act, M_P + 12 + c, i, M_NP)
                    upper(M_P + 16 + c, i, M_NP)
                    t = M_T + 20 + c
                    act.activation(zs[:, c, :], bank[t % RING][:], ACT.Silu).then_inc(taken[t % RING], 1)
                    if c == 2:
                        for d in range(MT):
                            act.wait_ge(hc_made, i * MT + (d + 1))
                            if d >= 2:
                                act.wait_ge(var_done, i * MT + (d - 1))
                            act.activation(sq[:, d % 2, :], xm[:, d, PAD:], ACT.Square).then_inc(msq_made, 1)
                act.wait_ge(var_done, (i + 1) * MT)
                act.activation(rstd[:], bank[6][:], ACT.Ln, bias=eps).then_inc(aux_free[6], 1)
                act.wait_ge(aux_free[6], AUX_M[6] + 2 + i * 2)
                act.activation(rstd[:], rstd[:], ACT.Exp, scale=-0.5).then_inc(mrs_made, 1)
                for d in range(MT):
                    act.wait_ge(y_made, i * MT + (d + 1))
                    act.activation(xm_hi[:, d, :], xm[:, d, PAD:], ACT.Copy).then_inc(yhi_made, 1)
                for e in range(4):
                    tile_full(act, M_P + 16 + e, i, M_NP)
                    upper(M_P + 20 + e, i, M_NP)

            def conv_out(i, c):
                act.wait_ge(conv_made, i * MT + (c + 1))
                act.activation(xc[:, c, :], xc[:, c, :], ACT.Silu).then_inc(xc_made, 1)
                act.wait_ge(xc_made, i * MT + (c + 1))
                act.activation(xc_hi[:, c, :], xc[:, c, :], ACT.Copy).then_inc(xchi_made, 1)
            steps.loop(MH, MT + NT, mlstm)

            square_x(4, lambda j: tile_taken(act, M_T + 3 * M_NT + 24 + j))
            norm_upper(3)
            lam = cols[:, 0, ROWS["r_lam_2"][1]:ROWS["r_lam_2"][1] + 12]
            link(act.activation(ctmp[:], lam, ACT.Abs))
            link(act.activation(ctmp[:], ctmp[:], ACT.Exp, scale=-1.0))
            link(act.activation(ctmp[:], ctmp[:], ACT.Ln, bias=1.0))
            act.sem_inc(c8_made, 1)
            for i in range(RG):
                p0, t0 = R_P + i * R_NP, R_T + i * R_NT
                act.wait_ge(gw_loaded, 256 * (i + 1))
                if i:
                    act.wait_ge(gw_used, 6 * i)
                for z in range(2):
                    act.activation(gw_hi[:, z].rearrange("p b c -> p (b c)"),
                                   gw[:, z].rearrange("p b c -> p (b c)"), ACT.Copy).then_inc(gw_hi_made, 1)
                for c in range(RT):
                    tile_full(act, p0 + c)
                    upper(p0 + c + 4)
                    act.activation(xr[:, c, PAD:], bank[(t0 + c) % RING][:], ACT.Copy)\
                       .then_inc(taken[(t0 + c) % RING], 1)
                for c in range(RT):
                    act.wait_ge(conv_made, MH * MT + i * RT + c + 1)
                    act.activation(rc_hi[:, c, :], rc[:, c, :], ACT.Copy).then_inc(rchi_made, 1)
                tile_full(act, p0 + 3)
                upper(p0 + 7)
                if i:
                    act.wait_ge(ry_made, RT * i)
                act.activation(rg[:, 0, :], bank[(t0 + 3) % RING][:], ACT.Silu).then_inc(taken[(t0 + 3) % RING], 1)
                act.wait_ge(c8_made, 2)
                for z, dst, b in ((0, rr, "r_b_a_2"), (1, ri, "r_b_x_2")):
                    for c in range(RT):
                        t = t0 + 4 + z * RT + c
                        act.wait_ge(gw_used, 6 * i + z * RT + c + 1)
                        act.activation(dst[:, c, :], bank[t % RING][:], ACT.Sigmoid,
                                       bias=col(b, i * RT + c)).then_inc(taken[t % RING], 1)
                for c in range(RT):
                    f = i * RT + c
                    tile_taken(act, t0 + 4 + c)
                    act.activation(rt[:, c, :], rr[:, c, :], ACT.Tanh, scale=c8[:, 1, f:f + 1])
                    act.activation(ra[:, c, :], rr[:, c, :], ACT.Exp, scale=c8[:, 0, f:f + 1]).then_inc(ra_made, 1)
                for c in range(RT):
                    act.wait_ge(rroot_in, i * RT + c + 1)
                    act.activation(rt[:, c, :], rt[:, c, :], ACT.Sqrt, scale=2.0).then_inc(rroot, 1)
                for c in (1, 2):
                    tile_full(act, p0 + 3 + c)
                    upper(p0 + 7 + c)
                    act.activation(rg[:, c, :], bank[(t0 + 9 + c) % RING][:], ACT.Silu)\
                       .then_inc(taken[(t0 + 9 + c) % RING], 1)
                for c in range(RT):
                    act.wait_ge(ry_made, i * RT + c + 1)
                    act.activation(y_hi[:, c, :], rh[:, c, :], ACT.Copy).then_inc(ryhi_made, 1)
                for e in range(4):
                    tile_full(act, p0 + 6 + e)
                    upper(p0 + 10 + e)
            square_x(5, lambda j: tile_taken(act, R_T + 3 * R_NT + 12 + j))
            for u in range(2 * NT):
                n, half = u // 2, u % 2
                if half == 0:
                    act.wait_ge(y_turned, u + 1)
                    act.activation(ytok[:, n, 0:512], bank[4 + u % 4][:], ACT.Copy).then_inc(aux_free[4 + u % 4], 1)
                    act.wait_ge(aux_free[4 + u % 4], AUX_E[4 + u % 4] + u // 4 + 1)
                    act.sem_inc(ytok_act, 1)

        @block.vector
        def _(dve):
            steps = Steps(dve, dve_steps)
            link = lambda ins: steps.link(ins)

            def split_low(dst, full, upper_half, sem_, made, *wait):
                dve.wait_ge(*wait)
                dve.tensor_tensor(dst, full, upper_half.bitcast(F32), ALU.subtract).then_inc(sem_, 1)

            def norm_apply(n, name, j0=0, norm=None):
                dve.wait_ge(rstd_made, (n if norm is None else norm) + 1)

                def lower(j):
                    dve.wait_ge(hi_made, DT * n + j + 1)
                    dve.tensor_tensor(h_lo[:, j, :], hf[:, j % 2, :], h_hi[:, j, :].bitcast(F32),
                                      ALU.subtract).then_inc(h_made, 1)
                for j in range(DT):
                    if j >= 2:
                        lower(j - 2)
                        dve.wait_ge(h_made, DT * n + j - 1)
                    dve.scalar_tensor_tensor(hf[:, j % 2, :], xT[:, j, :], col(name, j0 + j), rstd[:],
                                             ALU.mult, ALU.mult).then_inc(hf_made, 1)
                lower(DT - 2)
                lower(DT - 1)

            dve.memset(small[:, 0:1], EPS).then_inc(eps_made, 1)
            dve.wait_ge(consts, 1)
            dve.tensor_copy(mask_d[:], maskf[:, 0:1, :])
            for n in range(NT):
                dve.tensor_copy(mask4[:, 1:, n * 64:(n + 1) * 64], maskf[:, 1:, 0:64])
            for s in range(3):
                n = SHEET_ROWS[s]
                dve.wait_ge(turned, s + 1)
                dve.tensor_copy(cols[:, s, 0:n], bank[4 + s][:, 0:n]).then_inc(aux_free[4 + s], 1)
            dve.wait_ge(turned, 4)
            dve.tensor_copy(wsT[:].rearrange("p g q -> p (g q)"), bank[7][:]).then_inc(aux_free[7], 1)
            dve.wait_ge(aux_free[7], 1)
            link(dve.memset(wsT[64:P, :, 0:64], 0.0))
            for j in range(DT):
                dve.wait_ge(turned, 5 + j)
                dve.tensor_copy(xT[:, j, :], bank[4 + j % 4][:]).then_inc(aux_free[4 + j % 4], 1)
                dve.wait_ge(aux_free[4 + j % 4], 2 + j // 4)
                dve.sem_inc(x_made, 1)
            norm_apply(0, "norm_mix")

            for n in range(NT):
                dve.wait_ge(gv_turned, n + 1)
                link(dve.bn_stats(bn[:, n, 0:6], bank[4 + n][:]))
                link(dve.bn_aggr(bn[:, n, 6:8], bn[:, n, 0:6]))
            dve.sem_inc(var_made, 1)
            dve.wait_ge(rs_made, 1)
            dve.wait_ge(g_loaded, 64)
            for n in range(NT):
                dve.tensor_scalar(vn[:, n, :], bank[4 + n][:], bn[:, n, 6:7], small[:, 8 + n:9 + n],
                                  ALU.subtract, ALU.mult).then_inc(aux_free[4 + n], 1)
                dve.wait_ge(aux_free[4 + n], AUX_G[4 + n] + 1)
                link(dve.tensor_tensor(vn[:, n, :], vn[:, n, :], lng[:], ALU.mult))
                dve.tensor_tensor(vn[:, n, :], vn[:, n, :], lnb[:], ALU.add).then_inc(vn_made, 1)
            for g in range(GG):
                dve.wait_ge(mixed, g + 1)
                if g >= 2:
                    dve.wait_ge(ya_made, g - 1)
                view = yg[:, g % 2, :].rearrange("p (n q) -> p n q", q=P)
                dve.tensor_tensor(view, bank[4 + g][:].rearrange("p (n q) -> p n q", q=P),
                                  bsb[:, g:g + 1, :].to_broadcast([P, NT, P]), ALU.add).then_inc(aux_free[4 + g], 1)
                dve.wait_ge(aux_free[4 + g], AUX_G[4 + g] + 2)
                tile_taken(dve, G_T + 4 + g)
                dve.tensor_tensor(yg[:, g % 2, :], yg[:, g % 2, :], gu[:, g, :], ALU.mult).then_inc(yg_made, 1)
                dve.wait_ge(yg_hi, g + 1)
                dve.tensor_tensor(ya_lo[:, g, :], yg[:, g % 2, :], ya_hi[:, g, :].bitcast(F32),
                                  ALU.subtract).then_inc(ya_made, 1)

            dve.wait_ge(ya_made, GG)
            link(dve.memset(sd[:], 0.0))
            link(dve.memset(off[:], 0.0))

            def halves(ap, l):
                h = LEVELS[l]
                if h <= CHUNK:
                    v = ap.rearrange("p (b two s) -> p b two s", two=2, s=h)
                    return v[:, :, 0, :], v[:, :, 1, :]
                c = h // CHUNK
                v = ap.rearrange("p (b two c s) -> p b two c s", two=2, c=c, s=CHUNK)
                if h == 256:
                    return v[:, 0, 0], v[:, 0, 1]
                return v[:, :, 0], v[:, :, 1]

            def offsets(l):
                h = LEVELS[l]
                if h < CHUNK:
                    v = cum[:].rearrange("p (b two s) -> p b two s", two=2, s=h)[:, :, 0, h - 1:h]
                    v = v.to_broadcast([P, S // (2 * h), h])
                    return v, v
                row = off[:, l - 6, :]
                c = h // CHUNK
                if h == CHUNK:
                    v = row.rearrange("p (b two) -> p b two", two=2)
                    return (v[:, :, 0:1].to_broadcast([P, NCH // 2, CHUNK]),
                            v[:, :, 1:2].to_broadcast([P, NCH // 2, CHUNK]))
                if h == 256:
                    v = row.rearrange("p (two c) -> p two c", two=2)
                    return (v[:, 0, :].unsqueeze(2).to_broadcast([P, c, CHUNK]),
                            v[:, 1, :].unsqueeze(2).to_broadcast([P, c, CHUNK]))
                v = row.rearrange("p (b two c) -> p b two c", two=2, c=c)
                return (v[:, :, 0, :].unsqueeze(3).to_broadcast([P, 2, c, CHUNK]),
                        v[:, :, 1, :].unsqueeze(3).to_broadcast([P, 2, c, CHUNK]))

            def head_prepare(i):
                nl = len(LEVELS)
                dve.wait_ge(soft_made, i + 1)
                if not isinstance(i, int) or i > 0:
                    dve.wait_ge(level_done, i * NMASK)
                    dve.wait_ge(off_done, i)
                zf = bank[H_T % RING][:]
                link(dve.scalar_tensor_tensor(lf[:], zf, 0.0, lt[:], ALU.min, ALU.subtract))
                dve.tensor_tensor(kk[:], lf[:], zf, ALU.subtract).then_inc(taken[H_T % RING], 1)
                link(dve.tensor_tensor_scan(cum[:], keep[:], lf[:], 0.0, ALU.mult, ALU.add))
                last = cum[:].rearrange("p (c s) -> p c s", s=CHUNK)[:, :, CHUNK - 1]
                b0, b1, b2 = off[:, 0, :], off[:, 1, :], off[:, 2, :]
                dve.tensor_copy(b0[:, 0:8:2], last[:, 0:8:2])
                dve.tensor_tensor(b1[:, 0:8:4], last[:, 0:8:4], last[:, 1:8:4], ALU.add)
                dve.tensor_copy(b1[:, 1:8:4], last[:, 1:8:4])
                dve.tensor_copy(b1[:, 3:8:4], last[:, 2:8:4])
                link(dve.tensor_copy(b2[:, 3:6:2], last[:, 3:5]))
                link(dve.tensor_tensor(b2[:, 2:7:4], last[:, 2:6:3], b2[:, 3:6:2], ALU.add))
                link(dve.tensor_tensor(b2[:, 1:8:6], last[:, 1:7:5], b2[:, 2:7:4], ALU.add))
                link(dve.tensor_tensor(b2[:, 0:1], last[:, 0:1], b2[:, 1:2], ALU.add))

                def exponent(l):
                    e1, e2 = halves(ee[:, l % 3, :], l)
                    c1, c2 = halves(cum[:], l)
                    a1, a2 = offsets(l)
                    if l >= 3:
                        dve.wait_ge(qk_made, i * nl + (l - 2))
                    elif not isinstance(i, int) or i > 0:
                        dve.wait_ge(qk_made, i * nl)
                    dve.tensor_tensor(e1, a1, c1, ALU.subtract)
                    dve.tensor_tensor(e2, c2, a2, ALU.subtract if LEVELS[l] < CHUNK else ALU.add)\
                       .then_inc(expo_made, 1)

                def weigh(l):
                    dve.wait_ge(decay_made, i * nl + (l + 1))
                    if l == 0:
                        dve.wait_ge(k_made, i + 1)
                        tile_taken(dve, H_T + 1, i, H_N)
                    e1, e2 = halves(ee[:, l % 3, :], l)
                    o1, o2 = halves(qk[:, l, :], l)
                    k1, _ = halves(kk[:], l)
                    _, q2 = halves(qq[:], l)
                    dve.tensor_tensor(o1, e1, k1, ALU.mult)
                    dve.tensor_tensor(o2, e2, q2, ALU.mult).then_inc(qk_made, 1)
                exponent(0)
                exponent(1)
                for l in range(nl):
                    if l + 2 < nl:
                        exponent(l + 2)
                    weigh(l)

            def head_masks(i):
                turns = 0
                for m in range(NMASK):
                    b, at = M_BANK[m], M_AT[m]
                    dve.wait_ge(level_done, i * NMASK + (m + 2 if m in (1, 3, 5) else m + 1))
                    if m and m - 1 in M_FREED:
                        dve.wait_ge(aux_free[M_BANK[m - 1]], AUX_H[M_BANK[m - 1]] + M_FREED[m - 1]
                                    + i * H_AUX[M_BANK[m - 1]])
                    elif m:
                        dve.wait_ge(mask_turn, i * M_TURNS + turns)
                    dve.sem_inc(mask_turn, 1)
                    turns += 1
                    if m == 0:
                        dst, src = sd[:], bank[b][:].rearrange("p (n t) -> p n t", t=P)
                        mask = mask_d[:].to_broadcast([P, NT, P])
                    else:
                        h = LEVELS[m - 1]
                        nb = P // (2 * h)
                        dst = sd[:].rearrange("p n (b two t) -> p (n b) two t", two=2, t=h)[:, :, 1, :]
                        src = bank[b][:, at:at + 256].rearrange("p (nb t) -> p nb t", t=h)
                        mask = mask4[:, m, :].rearrange("p (nb t) -> p nb t", t=h)
                    ins = dve.copy_predicated(dst, mask, src)
                    if m in M_FREED:
                        ins.then_inc(aux_free[b], 1)
                    else:
                        ins.then_inc(mask_turn, 1)
                        turns += 1

            def head_out(i):
                dve.wait_ge(hrs_made, i + 1)
                dve.scalar_tensor_tensor(on, bank[6][:], col("hg_norm_g", 0), hrs, ALU.mult,
                                         ALU.mult).then_inc(aux_free[6], 1)
                dve.wait_ge(aux_free[6], AUX_H[6] + 2 + i * H_AUX[6])
                tile_taken(dve, H_T + 3, i, H_N)
                dve.tensor_tensor(on, on, zo, ALU.mult).then_inc(on_made, 1)
                dve.wait_ge(ohi_made, i + 1)
                pick = (lambda t: t[:, i, :]) if isinstance(i, int) else (
                    lambda t: t[:, bass.ds(i, 1), :].rearrange("p a s -> p (a s)"))
                dve.tensor_tensor(pick(o_lo), on, pick(o_hi).bitcast(F32), ALU.subtract).then_inc(olo_made, 1)

            head_prepare(0)

            def heads(i):
                head_masks(i)
                head_prepare(i + 1)
                head_out(i)
            steps.loop(HH - 1, 6, heads)
            head_masks(HH - 1)
            head_out(HH - 1)

            def ups(i):
                for e in range(2):
                    for z in range(2):
                        n = 4 * e + 2 * z
                        tile_taken(dve, U_T + n, i, U_N)
                        tile_full(dve, U_P + n + 1, i, U_N)
                        if z == 0:
                            dve.wait_ge(mix_made, i * 2 + (e + 1))
                        dve.tensor_tensor(gated[:, z, :], sg[:, z, :], bank[(U_T + n + 1) % RING][:],
                                          ALU.mult).then_inc(taken[(U_T + n + 1) % RING], 1)
                        tile_taken(dve, U_T + n + 1, i, U_N)
                    dve.tensor_tensor(gated[:, 0, :], gated[:, 0, :], gated[:, 1, :], ALU.add).then_inc(mixf_made, 1)
                    j = i * 2 + e
                    dve.wait_ge(mixhi_made, i * 2 + (e + 1))
                    pick = lambda t: t[:, bass.ds(j, 1), :].rearrange("p a s -> p (a s)")
                    dve.tensor_tensor(pick(mix_lo), gated[:, 0, :], pick(mix_hi).bitcast(F32),
                                      ALU.subtract).then_inc(mix_made, 1)
            dve.sem_inc(mix_made, 1)
            steps.loop(DT // 2, 0, ups)

            def add_x(j, p, t, i=0, per_p=0, per_t=0):
                tile_full(dve, p, i, per_p)
                dve.tensor_tensor(xT[:, j, :], xT[:, j, :], bank[t % RING][:], ALU.add).then_inc(taken[t % RING], 1)

            for j in range(DT):
                add_x(j, O_P + j, O_T + j)
            norm_apply(1, "norm_ffn")

            def ffn(i):
                for e in range(8):
                    tile_taken(dve, F_T + e, i, F_N)
                    if e >= 2:
                        dve.wait_ge(f_made, i * DT + (e - 1))
                    dve.tensor_tensor(ff[:, e % 2, :], fr[:, e % 2, :], fr[:, e % 2, :], ALU.mult).then_inc(ff_made, 1)
                    dve.wait_ge(fhi_made, i * DT + (e + 1))
                    dve.tensor_tensor(f_lo[:, e, :], ff[:, e % 2, :], f_hi[:, e, :].bitcast(F32),
                                      ALU.subtract).then_inc(f_made, 1)
                for e in range(8):
                    add_x(e, F_P + 8 + e, F_T + 8 + e, i, F_N, F_N)
            steps.loop(4, 0, ffn)
            
            dve.wait_ge(rstd_made, 3)
            for j in range(DT):
                dve.scalar_tensor_tensor(xT[:, j, :], xT[:, j, :], col("final_norm", j), rstd[:], ALU.mult,
                                         ALU.mult).then_inc(x_normed, 1)
            dve.wait_ge(gates_hi, 1)
            dve.tensor_tensor(wg_lo[:], wg[:], wg_hi[:].bitcast(F32), ALU.subtract).then_inc(gates_split, 1)
            norm_apply(2, "ln_g_2", 0, norm=3)
            link(dve.memset(gone[:], 1.0))
            dve.wait_ge(gsoft_made, 1)
            link(dve.scalar_tensor_tensor(gf[:], gf[:], 0.0, gt[:], ALU.min, ALU.subtract))
            link(dve.tensor_tensor_scan(gF[:], gone[:], gf[:], 0.0, ALU.mult, ALU.add))
            link(dve.tensor_tensor(gb[:], gi[:], gF[:], ALU.subtract))
            dve.sem_inc(gb_made, 1)
            link(dve.tensor_tensor_scan(gr[:], gb[:], gb[:], 0.0, ALU.max, ALU.max))
            link(dve.tensor_tensor(mst[:], gr[:], gF[:], ALU.add))
            link(dve.tensor_scalar(rneg, gr[:], -1.0, None, ALU.mult))
            dve.wait_ge(b_turned, 1)
            dve.tensor_copy(bcol[:].rearrange("p n h -> p (n h)"), bank[7][:, 0:NT * MH]).then_inc(aux_free[7], 1)
            dve.wait_ge(aux_free[7], AUX_MP[7] + 1)
            link(dve.memset(xm[:, :, 0:PAD], 0.0))

            s1, r1 = 1, 0
            w_at = ROWS["m_conv_w_2"][1]

            def mlstm(i):
                at = ROWS["m_conv_b_2"][1]
                dve.tensor_copy(mpar[:], cols[:, 1, 0:7 * 16].rearrange("p (k c) -> p k c", c=16)[
                    :, :, bass.ds(i * MT, MT)])
                dve.tensor_copy(bcur[:], bcol[:, :, bass.ds(i, 1)].rearrange("p n a -> p (n a)"))
                dve.tensor_copy(sel_cur[:], sel[:, bass.ds(i, 1), :].rearrange("p a c -> p (a c)"))\
                   .then_inc(head_set, 1)
                dve.wait_ge(head_set, i + 1)
                for c in range(MT):
                    dve.wait_ge(xmhi_made, i * MT + (c + 1))
                    dve.tensor_tensor(xm_lo[:, c, :], bank[(M_T + c) % RING][:], xm_hi[:, c, :].bitcast(F32),
                                      ALU.subtract).then_inc(taken[(M_T + c) % RING], 1)
                    link(dve.tensor_scalar(xc[:, c, :], xm[:, c, 1:1 + S], mpar[:, 0, c:c + 1],
                                           mpar[:, 4, c:c + 1], ALU.mult, ALU.add))
                    for j in (1, 2):
                        link(dve.scalar_tensor_tensor(xc[:, c, :], xm[:, c, 1 + j:1 + j + S], mpar[:, j, c:c + 1],
                                                      xc[:, c, :], ALU.mult, ALU.add))
                    dve.scalar_tensor_tensor(xc[:, c, :], xm[:, c, 4:4 + S], mpar[:, 3, c:c + 1],
                                             xc[:, c, :], ALU.mult, ALU.add).then_inc(conv_made, 1)
                    if c >= 1:
                        lower_xc(i, c - 1)
                tile_taken(dve, M_T + MT - 1, i, M_NT)
                dve.sem_inc(xm_made, MT)
                lower_xc(i, MT - 1)
                dve.wait_ge(aux_free[7], AUX_M[7] + 2 + i * 2)
                place_st = [0, 512, 896, 1152]
                sbank = [(4, 0), (5, 0), (6, 0), (6, 256)]

                def argument(n):
                    if n >= 2:
                        dve.wait_ge(st_made, i * NT + (n - 1))
                    dve.scalar_tensor_tensor(ww[:, n % 2, n * P:(n + 1) * P], nr[:, n * P:(n + 1) * P],
                                             bcur[:, n:n + 1], cap[:], ALU.add, ALU.min).then_inc(arg_made, 1)
                argument(0)
                argument(1)
                for n in range(NT):
                    b, at_ = sbank[n]
                    w = S - n * P
                    dve.wait_ge(w_made, i * NT + (n + 1))
                    dve.wait_ge(scores_done, i * NT + (n + 1 if n < 2 else NT))
                    dve.tensor_tensor(st[:, place_st[n]:place_st[n] + w], ww[:, n % 2, n * P:S],
                                      bank[b][:, at_:at_ + w], ALU.mult).then_inc(st_made, 1)
                    if n + 2 < NT:
                        argument(n + 2)
                dve.wait_ge(st_made, (i + 1) * NT)
                for b in (4, 5, 6):
                    dve.sem_inc(aux_free[b], 1)
                dve.wait_ge(aux_free[4], AUX_M[4] + 2 + i * 2)
                link(dve.tensor_tensor(den, den, enm, ALU.max))
                link(dve.reciprocal(den, den))
                for d in range(MT):
                    t = M_T + 16 + d
                    dve.wait_ge(num_done, i * MT + (d + 1))
                    dve.tensor_tensor(xm[:, d, PAD:], bank[t % RING][:], den, ALU.mult)\
                       .then_inc(taken[t % RING], 1)
                    tile_taken(dve, t, i, M_NT)
                    dve.tensor_tensor(xm[:, d, PAD:], xm[:, d, PAD:], og[:, d, :], ALU.mult).then_inc(hh_made, 1)
                dve.wait_ge(mean_done, i + 1)
                for d in range(MT):
                    dve.tensor_tensor(xm[:, d, PAD:], xm[:, d, PAD:], bank[5][:], ALU.subtract).then_inc(hc_made, 1)
                dve.wait_ge(hc_made, (i + 1) * MT)
                dve.sem_inc(aux_free[5], 1)
                dve.wait_ge(mrs_made, i + 1)
                for d in range(MT):
                    y = xm[:, d, PAD:]
                    link(dve.scalar_tensor_tensor(y, y, mpar[:, 5, d:d + 1], rstd[:], ALU.mult, ALU.mult))
                    link(dve.scalar_tensor_tensor(y, xc[:, d, :], mpar[:, 6, d:d + 1], y, ALU.mult, ALU.add))
                    tile_taken(dve, M_T + 20 + d, i, M_NT)
                    dve.tensor_tensor(y, y, zs[:, d, :], ALU.mult).then_inc(y_made, 1)
                    if d >= 1:
                        lower_y(i, d - 1)
                lower_y(i, MT - 1)
                for e in range(8):
                    add_x(e, M_P + 16 + e // 2, M_T + 24 + e, i, M_NP, M_NT)

            def lower_xc(i, c):
                dve.wait_ge(xchi_made, i * MT + (c + 1))
                dve.tensor_tensor(xc_lo[:, c, :], xc[:, c, :], xc_hi[:, c, :].bitcast(F32),
                                  ALU.subtract).then_inc(xcs_made, 1)

            def lower_y(i, d):
                dve.wait_ge(yhi_made, i * MT + (d + 1))
                dve.tensor_tensor(xm_lo[:, d, :], xm[:, d, PAD:], xm_hi[:, d, :].bitcast(F32),
                                  ALU.subtract).then_inc(ys_made, 1)
            steps.loop(MH, 3 * MT + 2 + 2 * MT, mlstm)

            tile_taken(dve, M_T + 4 * M_NT - 1)
            dve.memset(gw[:], 0.0).then_inc(gw_zero, 1)
            norm_apply(3, "ln_g_2", 8, norm=4)
            lam = cols[:, 0, ROWS["r_lam_2"][1]:ROWS["r_lam_2"][1] + 12]
            dve.wait_ge(c8_made, 1)
            link(dve.scalar_tensor_tensor(ctmp[:], lam, 0.0, ctmp[:], ALU.min, ALU.subtract))
            dve.tensor_scalar(c8[:, 0, :], ctmp[:], 8.0, None, ALU.mult)
            link(dve.tensor_scalar(c8[:, 1, :], ctmp[:], -8.0, None, ALU.mult))
            link(dve.memset(xr[:, :, 0:PAD], 0.0))
            dve.sem_inc(c8_made, 1)
            for i in range(RG):
                p0, t0 = R_P + i * R_NP, R_T + i * R_NT
                for z in range(2):
                    dve.wait_ge(gw_hi_made, 2 * i + z + 1)
                    dve.tensor_tensor(gw_lo[:, z].rearrange("p b c -> p (b c)"),
                                      gw[:, z].rearrange("p b c -> p (b c)"),
                                      gw_hi[:, z].rearrange("p b c -> p (b c)").bitcast(F32),
                                      ALU.subtract).then_inc(gw_split, 1)

                def lower(c):
                    dve.wait_ge(rchi_made, RT * i + c + 1)
                    dve.tensor_tensor(rc_lo[:, c, :], rc[:, c, :], rc_hi[:, c, :].bitcast(F32),
                                      ALU.subtract).then_inc(rcs_made, 1)
                for c in range(RT):
                    f = i * RT + c
                    tap = lambda j: cols[:, 2, j * 12 + f:j * 12 + f + 1]
                    tile_taken(dve, t0 + c)
                    link(dve.tensor_scalar(rc[:, c, :], xr[:, c, 1:1 + S], tap(0), col("r_conv_b_2", f),
                                           ALU.mult, ALU.add))
                    for j in (1, 2):
                        link(dve.scalar_tensor_tensor(rc[:, c, :], xr[:, c, 1 + j:1 + j + S], tap(j), rc[:, c, :],
                                                      ALU.mult, ALU.add))
                    dve.scalar_tensor_tensor(rc[:, c, :], xr[:, c, 4:4 + S], tap(3), rc[:, c, :],
                                             ALU.mult, ALU.add).then_inc(conv_made, 1)
                    if c:
                        lower(c - 1)
                lower(RT - 1)
                for c in range(RT):
                    u = ru[:, c % 2, :]
                    dve.wait_ge(ra_made, i * RT + c + 1)
                    link(dve.tensor_scalar(u, rt[:, c, :], 1.0, None, ALU.add))
                    link(dve.reciprocal(u, u))
                    dve.tensor_tensor(rt[:, c, :], rt[:, c, :], u, ALU.mult).then_inc(rroot_in, 1)
                    tile_taken(dve, t0 + 4 + RT + c)
                    link(dve.tensor_tensor(ri[:, c, :], ri[:, c, :], rc[:, c, :], ALU.mult))

                def lower_y(c):
                    dve.wait_ge(ryhi_made, RT * i + c + 1)
                    dve.tensor_tensor(y_lo[:, c, :], rh[:, c, :], y_hi[:, c, :].bitcast(F32),
                                      ALU.subtract).then_inc(rys_made, 1)
                for c in range(RT):
                    dve.wait_ge(rroot, i * RT + c + 1)
                    link(dve.tensor_tensor(ri[:, c, :], ri[:, c, :], rt[:, c, :], ALU.mult))
                    link(dve.tensor_tensor_scan(rh[:, c, :], ra[:, c, :], ri[:, c, :], 0.0, ALU.mult, ALU.add))
                    tile_taken(dve, t0 + 3 if c == 0 else t0 + 9 + c)
                    dve.tensor_tensor(rh[:, c, :], rh[:, c, :], rg[:, c, :], ALU.mult).then_inc(ry_made, 1)
                    if c:
                        lower_y(c - 1)
                lower_y(RT - 1)
                for e in range(8):
                    add_x(e, p0 + 6 + e // 2, t0 + 12 + e)
            dve.wait_ge(rstd_made, 6)
            for j in range(DT):
                dve.scalar_tensor_tensor(yf[:, j, :], xT[:, j, :], col("final_g_2", j), rstd[:], ALU.mult,
                                         ALU.mult).then_inc(yf_made, 1)
            for u in range(1, 2 * NT, 2):
                dve.wait_ge(y_turned, u + 1)
                dve.tensor_copy(ytok[:, u // 2, 512:1024], bank[4 + u % 4][:]).then_inc(aux_free[4 + u % 4], 1)
                dve.wait_ge(aux_free[4 + u % 4], AUX_E[4 + u % 4] + u // 4 + 1)
                dve.sem_inc(ytok_dve, 1)


_INS = [
    "x", "w_in", "gmlp_ln_g", "gmlp_ln_b", "gmlp_ws", "gmlp_bs", "w_up_a", "hg_norm_g", "w_up_b", "w_out", "norm_mix",
    "norm_ffn", "w_ff1", "w_ff2", "final_norm", "ln_g_2", "final_g_2", "m_w_in_2", "m_conv_w_2", "m_conv_b_2",
    "m_w_q_2", "m_w_k_2", "m_w_v_2", "m_b_i_2", "m_b_f_2", "m_norm_w_2", "m_skip_2", "m_w_out_2", "r_w_in_2",
    "r_conv_w_2", "r_conv_b_2", "r_w_a_2", "r_b_a_2", "r_w_x_2", "r_b_x_2", "r_lam_2", "r_w_out_2",
]


def kernel(**inputs):
    import numpy as np
    import concourse.bacc as bacc
    from concourse.bass_utils import run_bass_kernel_spmd

    nc = bacc.Bacc("TRN2", target_bir_lowering=False, num_devices=1)
    arrays, args = {}, {}
    for name in _INS:
        a = np.ascontiguousarray(inputs[name])
        arrays[f"in_{name}"] = a
        args[name] = nc.dram_tensor(f"in_{name}", a.shape, mybir.dt.from_np(a.dtype), kind="ExternalInput").ap()
    out = nc.dram_tensor("out", (1, S, D), F32, kind="ExternalOutput").ap()
    two_blocks(nc, args, out)
    r = run_bass_kernel_spmd(nc, [arrays], core_ids=[0])
    return r.results[0]["out"]
```
